# Optimizing a Trainium2 kernel written in Bass

```python
import math
import jax, jax.numpy as jnp
from jax import lax
import numpy as np

D_MODEL = 1024
BATCH = 1
SEQ = 1024
DEPTH = 2

CHUNK = 64
N_MIXERS = 2
N_SB_LAYERS = (DEPTH + 1) // 2
N_CV_LAYERS = DEPTH // 2
SB_HEADS = 16
SB_HEAD_DIM = D_MODEL // SB_HEADS
Q_BLOCK = 128
CONV_WIDTH = 31
N_EXPERTS = 16
N_GROUPS = 4
EXPERTS_PER_GROUP = N_EXPERTS // N_GROUPS
TOP_K = 2
D_EXPERT = 512
EXPERT_BLOCK = 256
NORM_EPS = 1e-6

kernel_name = "hybrid_stickbreak_conformer_groupmoe"

def rms_norm(x, g):
    xf = x.astype(jnp.float32)
    y = xf * lax.rsqrt(jnp.mean(xf * xf, axis=-1, keepdims=True) + NORM_EPS)
    return (y * g.astype(jnp.float32)).astype(x.dtype)

def layer_norm(x, g, b):
    xf = x.astype(jnp.float32)
    mu = jnp.mean(xf, axis=-1, keepdims=True)
    var = jnp.mean(jnp.square(xf - mu), axis=-1, keepdims=True)
    y = (xf - mu) * lax.rsqrt(var + NORM_EPS) * g.astype(jnp.float32) + b.astype(jnp.float32)
    return y.astype(x.dtype)

def modulate(h, shift, scale):
    return h * (1 + scale[:, None, :]) + shift[:, None, :]

def stick_breaking_attention(q, k, v):
    S = q.shape[2]
    inv_sqrt_d = 1.0 / math.sqrt(q.shape[-1])
    outs = []
    for qb in range(S // Q_BLOCK):
        q0, q1 = qb * Q_BLOCK, (qb + 1) * Q_BLOCK
        qi = q[:, :, q0:q1]
        kj = k[:, :, :q1]
        vj = v[:, :, :q1]
        z = jnp.einsum('bhqd,bhkd->bhqk', qi, kj).astype(jnp.float32) * inv_sqrt_d
        t_idx = q0 + jnp.arange(Q_BLOCK)[:, None]
        s_idx = jnp.arange(q1)[None, :]
        mask = s_idx < t_idx
        log_beta = jax.nn.log_sigmoid(z)
        log_1m_beta = jnp.where(mask, jax.nn.log_sigmoid(-z), 0.0)
        acc = lax.cumsum(log_1m_beta, axis=3, reverse=True) - log_1m_beta
        a = jnp.where(mask, jnp.exp(log_beta + acc), 0.0)
        outs.append(jnp.einsum('bhqk,bhkd->bhqd', a.astype(v.dtype), vj))
    return jnp.concatenate(outs, axis=2)

def stick_breaking_mixer(h, w_qkv, w_o):
    B, S, D = h.shape
    qkv = (h @ w_qkv).reshape(B, S, 3, SB_HEADS, SB_HEAD_DIM)
    q = qkv[:, :, 0].transpose(0, 2, 1, 3)
    k = qkv[:, :, 1].transpose(0, 2, 1, 3)
    v = qkv[:, :, 2].transpose(0, 2, 1, 3)
    o = stick_breaking_attention(q, k, v).transpose(0, 2, 1, 3).reshape(B, S, D)
    return o @ w_o

def conformer_conv_module(h, w_in, b_in, w_dw, b_dw, ln_g, ln_b, w_out, b_out):
    D = h.shape[-1]
    u = h @ w_in + b_in
    u = u[..., :D] * jax.nn.sigmoid(u[..., D:])
    u = lax.conv_general_dilated(
        u, w_dw[:, None, :].astype(u.dtype),
        window_strides=(1,), padding=[(CONV_WIDTH - 1, 0)],
        dimension_numbers=('NWC', 'WIO', 'NWC'), feature_group_count=D) + b_dw
    u = jax.nn.silu(layer_norm(u, ln_g, ln_b))
    return u @ w_out + b_out

def route(hf, w_router, b_router):
    T = hf.shape[0]
    scores = jax.nn.sigmoid((hf @ w_router).astype(jnp.float32))
    sel = scores + b_router.astype(jnp.float32)
    sel_g = sel.reshape(T, N_GROUPS, EXPERTS_PER_GROUP)
    group_score = jnp.sum(lax.top_k(sel_g, TOP_K)[0], axis=-1)
    g = jnp.argmax(group_score, axis=-1)
    in_group = jnp.take_along_axis(sel_g, g[:, None, None], axis=1)[:, 0]
    _, local = lax.top_k(in_group, TOP_K)
    idx = g[:, None] * EXPERTS_PER_GROUP + local
    w = jnp.take_along_axis(scores, idx, axis=1)
    w = w / jnp.sum(w, axis=-1, keepdims=True)
    return idx.astype(jnp.int32), w

def moe_ffn(h, w_router, b_router, w_gate, w_up, w_down):
    B, S, D = h.shape
    T = B * S
    TK = T * TOP_K
    hf = h.reshape(T, D)
    idx, wts = route(hf, w_router, b_router)
    flat_e = idx.reshape(-1)
    flat_tok = jnp.repeat(jnp.arange(T, dtype=jnp.int32), TOP_K)
    flat_w = wts.reshape(-1)
    counts = jax.ops.segment_sum(jnp.ones((TK,), jnp.int32), flat_e, num_segments=N_EXPERTS)
    padded = (counts + EXPERT_BLOCK - 1) // EXPERT_BLOCK * EXPERT_BLOCK
    pad_end = jnp.cumsum(padded)
    pad_start = pad_end - padded
    start = jnp.cumsum(counts) - counts
    order = jnp.argsort(flat_e)
    se = flat_e[order]
    dest = pad_start[se] + (jnp.arange(TK, dtype=jnp.int32) - start[se])
    n_rows = TK + N_EXPERTS * EXPERT_BLOCK
    n_blk = n_rows // EXPERT_BLOCK
    row_tok = jnp.full((n_rows,), T, jnp.int32).at[dest].set(flat_tok[order])
    row_w = jnp.zeros((n_rows,), jnp.float32).at[dest].set(flat_w[order])
    blk_e = jnp.minimum(jnp.searchsorted(pad_end, jnp.arange(n_blk) * EXPERT_BLOCK, side='right'),
                        N_EXPERTS - 1).astype(jnp.int32)
    h_pad = jnp.concatenate([hf, jnp.zeros((1, D), hf.dtype)], axis=0)
    xb = h_pad[row_tok].reshape(n_blk, EXPERT_BLOCK, D)

    def expert_block(args):
        xe, e = args
        return (jax.nn.silu(xe @ w_gate[e]) * (xe @ w_up[e])) @ w_down[e]

    yb = lax.map(expert_block, (xb, blk_e)).reshape(n_rows, D)
    y = jnp.zeros((T + 1, D), yb.dtype).at[row_tok].add(yb * row_w[:, None].astype(yb.dtype))
    return y[:T].reshape(B, S, D)

def setup_inputs(seed: int = 0) -> dict:
    key = jax.random.key(seed)
    ks = jax.random.split(key, 24)
    D, F, E = D_MODEL, D_EXPERT, N_EXPERTS
    nrm = lambda k, shape, s: jax.random.normal(k, shape, jnp.float32) * s
    return {
        "x": nrm(ks[0], (BATCH, SEQ, D), 1.0),
        "c": nrm(ks[1], (BATCH, D), 1.0),
        "norm1_g": 1.0 + nrm(ks[2], (DEPTH, D), 0.02),
        "norm2_g": 1.0 + nrm(ks[3], (DEPTH, D), 0.02),
        "w_ada": nrm(ks[4], (DEPTH, D, 6 * D), 0.5 * D ** -0.5),
        "b_ada": nrm(ks[5], (DEPTH, 6 * D), 0.02),
        "sb_w_qkv": nrm(ks[6], (N_SB_LAYERS, D, 3 * D), D ** -0.5),
        "sb_w_o": nrm(ks[7], (N_SB_LAYERS, D, D), D ** -0.5),
        "cv_w_in": nrm(ks[8], (N_CV_LAYERS, D, 2 * D), D ** -0.5),
        "cv_b_in": nrm(ks[9], (N_CV_LAYERS, 2 * D), 0.02),
        "cv_w_dw": nrm(ks[10], (N_CV_LAYERS, CONV_WIDTH, D), CONV_WIDTH ** -0.5),
        "cv_b_dw": nrm(ks[11], (N_CV_LAYERS, D), 0.02),
        "cv_ln_g": 1.0 + nrm(ks[12], (N_CV_LAYERS, D), 0.02),
        "cv_ln_b": nrm(ks[13], (N_CV_LAYERS, D), 0.02),
        "cv_w_out": nrm(ks[14], (N_CV_LAYERS, D, D), D ** -0.5),
        "cv_b_out": nrm(ks[15], (N_CV_LAYERS, D), 0.02),
        "w_router": nrm(ks[16], (D, E), D ** -0.5),
        "b_router": nrm(ks[17], (E,), 0.01),
        "moe_w_gate": nrm(ks[18], (DEPTH, E, D, F), D ** -0.5),
        "moe_w_up": nrm(ks[19], (DEPTH, E, D, F), D ** -0.5),
        "moe_w_down": nrm(ks[20], (DEPTH, E, F, D), F ** -0.5),
        "final_g": 1.0 + nrm(ks[21], (D,), 0.02),
    }

def reference(x, c, norm1_g, norm2_g, w_ada, b_ada, sb_w_qkv, sb_w_o,
              cv_w_in, cv_b_in, cv_w_dw, cv_b_dw, cv_ln_g, cv_ln_b, cv_w_out, cv_b_out,
              w_router, b_router, moe_w_gate, moe_w_up, moe_w_down, final_g):
    cond = jax.nn.silu(c)
    for layer in range(DEPTH):
        mod = cond @ w_ada[layer] + b_ada[layer]
        sh1, sc1, g1, sh2, sc2, g2 = jnp.split(mod, 6, axis=-1)
        h = modulate(rms_norm(x, norm1_g[layer]), sh1, sc1)
        j = layer // N_MIXERS
        if layer % N_MIXERS == 0:
            y = stick_breaking_mixer(h, sb_w_qkv[j], sb_w_o[j])
        else:
            y = conformer_conv_module(h, cv_w_in[j], cv_b_in[j], cv_w_dw[j], cv_b_dw[j],
                                      cv_ln_g[j], cv_ln_b[j], cv_w_out[j], cv_b_out[j])
        x = x + g1[:, None, :] * y
        h = modulate(rms_norm(x, norm2_g[layer]), sh2, sc2)
        x = x + g2[:, None, :] * moe_ffn(h, w_router, b_router,
                                        moe_w_gate[layer], moe_w_up[layer], moe_w_down[layer])
    return rms_norm(x, final_g)


_drawn_inputs = setup_inputs


def setup_inputs(seed=0):
    import zlib

    import numpy as np

    out = dict(_drawn_inputs(seed))
    spreads = {}
    factors = {'cv_b_in': 4.233,
     'cv_b_dw': 3.283,
     'cv_ln_g': 3.633,
     'cv_ln_b': 4.353,
     'cv_b_out': 3.555,
     'final_g': 2.75}
    for name, (base, spread) in spreads.items():
        noise = np.random.default_rng([zlib.crc32(name.encode()), seed]).standard_normal(out[name].shape)
        drawn = base * np.exp(spread * noise) if base else spread * noise
        out[name] = __import__('jax').numpy.asarray(drawn.astype(out[name].dtype))
    for name, factor in factors.items():
        out[name] = (out[name] * factor).astype(out[name].dtype)
    return out
```

```python
from contextlib import ExitStack

import concourse.bass as bass
from concourse import mybir

P = 128
T, D, F, E = 1024, 1024, 512, 16
HEADS, HD = 16, 64
TT, DC = T // P, D // P
GROUPS, EPG = 4, 4
CW = 31
EPS = 1e-6
PIECE = DC * 512
ADA = 12
MAXBLK = 32
TABLE = MAXBLK + 2
ADD_TAPS = 8


def trunk(nc, x, c_col, b_ada, norm_g, vec_cols, b_out, b_router, w_router, w_ada, w_qkv, w_o, w_in, w_out,
          w_gate, w_up, w_down, out):
    f32, i32 = mybir.dt.float32, mybir.dt.int32
    ALU, ACT, AX = mybir.AluOpType, mybir.ActivationFunctionType, mybir.AxisListType
    ds = bass.ds

    mod_dram = nc.dram_tensor("mod_rows", (2 * 6 * D,), f32, kind="Internal").ap()
    h_dram = [nc.dram_tensor(f"h_rows{l}", (T, D), f32, kind="Internal").ap() for l in range(2)]
    y_dram = [nc.dram_tensor(f"expert_rows{l}", (MAXBLK * P, D), f32, kind="Internal").ap() for l in range(2)]
    tok_dram = [nc.dram_tensor(f"slot_token{l}", (TABLE * P, 1), f32, kind="Internal").ap() for l in range(2)]

    ctx = ExitStack()
    with ctx:
        def sb(name, shape, dt=f32):
            return ctx.enter_context(nc.sbuf_tensor(name, shape, dt))

        def sem(name):
            return ctx.enter_context(nc.semaphore(name))

        xq = sb("xq", [P, TT, DC, P])
        kv = sb("kv", [P, 4 * PIECE])
        hT = sb("hT", [P, DC, T])
        ring = sb("ring", [P, 3, PIECE])
        bcA, bcB, bcC = sb("bcA", [P, D]), sb("bcB", [P, D]), sb("bcC", [P, D])
        pbuf = sb("pbuf", [P, 2, D + 2])
        oT = sb("oT", [P, DC, P])
        ident, ones, upper = sb("ident", [P, P]), sb("ones", [P, P]), sb("upper", [P, P])
        before, half_ones = sb("before", [P, P]), sb("half_ones", [P, 2, P])
        qstage = sb("qstage", [P, 2, P])
        cols = sb("cols", [P, 296 + 8])
        cond = sb("cond", [P, DC])
        wr = sb("wr", [P, DC, E])
        brt = sb("brt", [P, E])
        ss, rstd = sb("ss", [P, TT]), sb("rstd", [P, TT])
        tokid = sb("tokid", [P, TT])
        pref_e, pref_g = sb("pref_e", [P, TT, E]), sb("pref_g", [P, TT, GROUPS])
        dest = sb("dest", [P, 2, TT], i32)
        wts = sb("wts", [P, 2, TT])
        bounds = sb("bounds", [1, E + 1], i32)
        slot_row = sb("slot_row", [TABLE, P])
        slot_tok = sb("slot_tok", [P, TABLE], i32)
        idx_now = sb("idx_now", [P, 1], i32)

        iota_i = qstage[:, 0, :].bitcast(i32)
        ccol = cols[:, 0:8]
        b_in_c, w_dw_c = cols[:, 8:24], cols[:, 24:24 + 248].rearrange("p (c k) -> p c k", c=DC)
        b_dw_c, ln_g_c, ln_b_c = cols[:, 272:280], cols[:, 280:288], cols[:, 288:296]

        kT = kv[:, 0:2 * PIECE].rearrange("p (c t) -> p c t", c=DC)
        vt = kv[:, 2 * PIECE:4 * PIECE].rearrange("p (s f) -> p s f", s=TT)
        beta, omega, prob, probT = hT[:, 0:2, :], hT[:, 2:4, :], hT[:, 4:6, :], hT[:, 6:8, :]
        cv = kT
        UW = T + CW - 1
        upad = kv[:, 2 * PIECE:2 * PIECE + 2 * UW].rearrange("p (b t) -> p b t", b=2)
        o_ = 2 * PIECE + 2 * UW
        usig = kv[:, o_:o_ + 2 * T].rearrange("p (b t) -> p b t", b=2)
        tapp = kv[:, o_ + 2 * T:o_ + 4 * T].rearrange("p (b t) -> p b t", b=2)
        acc2 = kv[:, o_ + 4 * T:o_ + 5 * T]
        hflat = hT[:, :, :].rearrange("p c t -> p (c t)")
        xg, xT = hflat[:, 0:1024], hflat[:, 1024:2048].rearrange("p (c t) -> p c t", c=DC)
        sg, ha, haT = hflat[:, 2048:2560], hflat[:, 2560:3072], hflat[:, 3072:3584]
        yo = hflat[:, 3584:4608]
        wset = [[ring[:, k, :] for k in range(3)], [kv[:, k * PIECE:(k + 1) * PIECE] for k in range(3)]]
        spare = kv[:, 3 * PIECE:4 * PIECE]
        ygat = spare.rearrange("p (b k d) -> p b k d", b=2, k=2)

        def tmp(n, w=E):
            return spare[:, n * P:n * P + TT * w].rearrange("p (t e) -> p t e", t=TT)

        ps = ctx.enter_context(nc.psum_tensor("ps", [P, 8 * 512], f32))

        def bank(b, n=1):
            return ps[:, 512 * b:512 * (b + n)]

        const_made = sem("const_made")
        x_loaded, cols_loaded = sem("x_loaded"), sem("cols_loaded")
        cond_made = sem("cond_made")
        zeros_made, zeros_stored = sem("zeros_made"), sem("zeros_stored")
        slot_loaded = [sem(f"slot_loaded{k}") for k in range(3)]
        ada_used, ada_row, mod_stored = sem("ada_used"), sem("ada_row"), sem("mod_stored")
        bc_loaded, gate_loaded, a_made = sem("bc_loaded"), sem("gate_loaded"), sem("a_made")
        sq_done, ms_done, root_done, rstd_done = sem("sq_done"), sem("ms_done"), sem("root_done"), sem("rstd_done")
        h_scaled, h_made, h_turned, h_kept, h_stored = (sem("h_scaled"), sem("h_made"), sem("h_turned"),
                                                        sem("h_kept"), [sem(f"h_stored{b}") for b in range(2)])
        at_loaded = [sem(f"at_loaded{j}") for j in range(8)]
        proj_done, proj_kept = sem("proj_done"), sem("proj_kept")
        q_staged, z_done, sig_done, masked, scanned = (sem("q_staged"), sem("z_done"), sem("sig_done"),
                                                       sem("masked"), sem("scanned"))
        prob_made, prob_turned, probT_kept, av_done, o_kept = (sem("prob_made"), sem("prob_turned"),
                                                               sem("probT_kept"), sem("av_done"), sem("o_kept"))
        o_turned, oT_kept, wo_done, wo_scaled, x_again, x_made = (sem("o_turned"), sem("oT_kept"), sem("wo_done"),
                                                                  sem("wo_scaled"), sem("x_again"), sem("x_made"))
        edge_ready = sem("edge_ready")
        cv_loaded = [sem(f"cv_loaded{j}") for j in range(6)]
        in_done, usig_done, u_done, tap_made, tap_added, conv_done = (
            sem("in_done"), sem("usig_done"), sem("u_done"), sem("tap_made"), sem("tap_added"), sem("conv_done"))
        first_tap, dve_tap = sem("first_tap"), sem("dve_tap")
        mean_done, centered, squared, var_done, ln_root, ln_rstd, ln_scaled, ln_done = (
            sem("mean_done"), sem("centered"), sem("squared"), sem("var_done"), sem("ln_root"), sem("ln_rstd"),
            sem("ln_scaled"), sem("ln_done"))
        bout_loaded, out_done, out_used = sem("bout_loaded"), sem("out_done"), sem("out_used")
        both = lambda name: [sem(f"{name}{l}") for l in range(2)]
        logits_done, score_done, picked, counted, dest_made = (
            both("logits_done"), both("score_done"), both("picked"), both("counted"), both("dest_made"))
        bounds_made, table_filled, table_read, table_turned, table_made = (
            both("bounds_made"), both("table_filled"), both("table_read"),
            both("table_turned"), both("table_made"))
        w_loaded = [[[sem(f"w_loaded{l}{s}{k}") for k in range(3)] for s in range(2)] for l in range(2)]
        x_gathered, x_turned, xT_kept = both("x_gathered"), both("x_turned"), both("xT_kept")
        gate_done, up_done, silu_done, ha_made, ha_turned, haT_kept = (
            both("gate_done"), both("up_done"), both("silu_done"), both("ha_made"), both("ha_turned"), both("haT_kept"))
        down_done, y_kept = both("down_done"), both("y_kept")
        stored = both("stored")
        y_gathered = [[sem(f"y_gathered{l}{b}") for b in range(2)] for l in range(2)]
        x_added = both("x_added")
        dve_step = sem("dve_step")
        final_made, out_stored = sem("final_made"), [sem(f"out_stored{b}") for b in range(2)]

        block = ctx.enter_context(nc.Block())

        MOD = [(0, 0, 1, 2), (0, 3, 4, 5), (1, 0, 1, 2), (1, 3, 4, 5)]

        def mod_row(l, j):
            return mod_dram[(6 * l + j) * D:(6 * l + j + 1) * D].partition_broadcast(P)

        @block.sync
        def _(sp):
            sp.dma_start(xq[:, :, :, :].rearrange("p t c j -> p t (c j)"),
                         x.rearrange("(t p) d -> p t d", p=P)).then_inc(x_loaded, 16)
            for k in range(3):
                sp.dma_start(ring[:, k, :], w_ada[k]).then_inc(slot_loaded[k], 16)
            with sp.Fori(1, 2 * ADA // 3) as i:
                for k in range(3):
                    sp.wait_ge(ada_used, 3 * i + k - 2)
                    sp.dma_start(ring[:, k, :], w_ada[ds(3 * i + k, 1)].rearrange("a p n -> (a p) n")).then_inc(
                        slot_loaded[k], 16)
            for j in range(8):
                if j < 3:
                    sp.wait_ge(ada_used, 2 * ADA - 2 + j)
                else:
                    sp.wait_ge(proj_done, (4, 8, 12, 16, 32)[j - 3])
                sp.dma_start(ring[:, j % 3, :], w_qkv[j] if j < 6 else w_o[j - 6]).then_inc(at_loaded[j], 16)
                if j == 2:
                    sp.wait_ge(zeros_made, 1)
                    for l in range(2):
                        sp.dma_start(y_dram[l][E * P:, :].rearrange("(b p) d -> p b d", p=P),
                                     spare[:, 0:D].unsqueeze(1).to_broadcast([P, MAXBLK - E, D])).then_inc(
                                         zeros_stored, 16)

            def experts(l, set0_free, set1_free):
                for s, free in ((0, set0_free), (1, set1_free)):
                    for k, w in enumerate((w_gate, w_up, w_down)):
                        if k == 0:
                            free()
                        sp.dma_start(wset[s][k], w[l * E + s]).then_inc(w_loaded[l][s][k], 16)
                sp.wait_ge(bounds_made[l], 1)
                with sp.Fori(1, E // 2) as i:
                    for s in range(2):
                        ends = sp.value_load(bounds[0:1, ds(2 * i + s - 1, 1)], min_val=1, max_val=MAXBLK)
                        sp.wait_ge(down_done[l], 2 * ends)
                        for k, w in enumerate((w_gate, w_up, w_down)):
                            sp.dma_start(wset[s][k], w[ds(2 * i + s + l * E, 1)].rearrange("a p n -> (a p) n")
                                         ).then_inc(w_loaded[l][s][k], 16)
                last = sp.value_load(bounds[0:1, E:E + 1], min_val=1, max_val=MAXBLK)
                sp.wait_ge(down_done[l], 2 * last)

            experts(0, lambda: sp.wait_ge(wo_done, TT), lambda: sp.wait_ge(x_made, TT))
            for j in range(6):
                if j >= 3:
                    sp.wait_ge(in_done, (4, 4, 8)[j - 3])
                sp.dma_start(ring[:, j % 3, :], w_in[j] if j < 4 else w_out[j - 4]).then_inc(cv_loaded[j], 16)
            experts(1, lambda: sp.wait_ge(out_done, 2 * TT), lambda: sp.wait_ge(out_done, 2 * TT))
            for t in range(TT):
                sp.wait_ge(final_made, t + 1)
                sp.dma_start(out[t * P:(t + 1) * P, :], pbuf[:, t % 2, 0:D]).then_inc(out_stored[t % 2], 16)
            for b in range(2):
                sp.wait_ge(out_stored[b], 16 * TT // 2)

        @block.gpsimd
        def _(pool):
            kvrow = kv[0:1, 0:2 * 6 * D]
            pool.dma_start(cols[:, :], vec_cols).then_inc(cols_loaded, 16)
            pool.dma_start(kvrow, b_ada).then_inc(cols_loaded, 16)
            pool.dma_start(wr[:, :, :], w_router).then_inc(cols_loaded, 16)
            pool.dma_start(brt[:, :], b_router.partition_broadcast(P)).then_inc(cols_loaded, 16)
            nc.gpsimd.memset(ident[:, :], 0.0)
            nc.gpsimd.memset(upper[:, :], 1.0)
            nc.gpsimd.memset(ones[:, :], 1.0)
            nc.gpsimd.memset(before[:, :], 1.0)
            nc.gpsimd.memset(slot_row[:, :], 0.0)
            nc.gpsimd.memset(pbuf[:, :, D:D + 2], 1.0)
            nc.gpsimd.memset(half_ones[:, :, :], 1.0).then_inc(const_made, 1)
            pool.wait_ge(const_made, 1)
            nc.gpsimd.affine_select(out=ident[:, :], in_=ident[:, :], compare_op=ALU.not_equal, fill=1.0, base=0,
                                    pattern=[[-1, P]], channel_multiplier=1)
            nc.gpsimd.affine_select(out=half_ones[:, 0, :], in_=half_ones[:, 0, :], compare_op=ALU.is_gt, fill=0.0,
                                    base=HD, pattern=[[0, P]], channel_multiplier=-1)
            nc.gpsimd.affine_select(out=half_ones[:, 1, :], in_=half_ones[:, 1, :], compare_op=ALU.is_ge, fill=0.0,
                                    base=-HD, pattern=[[0, P]], channel_multiplier=1)
            nc.gpsimd.affine_select(out=before[:, :], in_=before[:, :], compare_op=ALU.is_gt, fill=0.0, base=0,
                                    pattern=[[-1, P]], channel_multiplier=1)
            nc.gpsimd.affine_select(out=upper[:, :], in_=upper[:, :], compare_op=ALU.is_gt, fill=0.0, base=0,
                                    pattern=[[1, P]], channel_multiplier=-1).then_inc(const_made, 1)
            for n, (pattern, base, mul, width) in enumerate((([[P, TT]], 0, 1, TT), ([[0, TT], [-1, GROUPS]], GROUPS, 0,
                                                              TT * GROUPS), ([[0, TT], [-1, E]], E, 0, TT * E))):
                if n:
                    pool.wait_ge(dve_step, n)
                nc.gpsimd.iota(iota_i[:, 0:width], pattern=pattern, base=base, channel_multiplier=mul).then_inc(
                    const_made, 1)
            for l in range(2):
                pool.dma_start(tok_dram[l].rearrange("(b p) a -> b (p a)", p=P), slot_row[:, :]).then_inc(
                    stored[l], 16)
            pool.wait_ge(ada_row, 2 * ADA)
            pool.dma_start(mod_dram.unsqueeze(0), kvrow).then_inc(mod_stored, 16)
            pool.wait_ge(mod_stored, 16)

            def norm(n, free):
                l, shift, scale, gate = MOD[n]
                free()
                pool.dma_start(bcA[:, :], mod_row(l, scale)).then_inc(bc_loaded, 16)
                pool.dma_start(bcB[:, :], mod_row(l, shift)).then_inc(bc_loaded, 16)
                pool.dma_start(bcC[:, :], norm_g[n].partition_broadcast(P)).then_inc(bc_loaded, 16)
                pool.wait_ge(a_made, n + 1)
                pool.dma_start(bcC[:, :], mod_row(l, gate)).then_inc(gate_loaded, 16)
                if n % 2:
                    for t in range(TT):
                        pool.wait_ge(h_made, TT * n + t + 1)
                        pool.dma_start(h_dram[l][t * P:(t + 1) * P, :], pbuf[:, t % 2, 0:D]).then_inc(
                            h_stored[t % 2], 16)

            norm(0, lambda: None)

            def stage(qb, chunk, u):
                nc.gpsimd.tensor_tensor(qstage[:, u, :], xq[:, qb, ds(chunk, 1), :].rearrange("p a t -> p (a t)"),
                                        half_ones[:, u, :], ALU.mult).then_inc(q_staged, 1)

            def mask(qb, g, u):
                pool.wait_ge(sig_done, g + 1)
                diag = slice(qb * P, (qb + 1) * P)
                nc.gpsimd.tensor_tensor(beta[:, u, diag], beta[:, u, diag], before[:, :], ALU.mult)
                nc.gpsimd.affine_select(out=omega[:, u, diag], in_=omega[:, u, diag], compare_op=ALU.is_gt, fill=1.0,
                                        base=0, pattern=[[-1, P]], channel_multiplier=1).then_inc(masked, 1)

            pool.wait_ge(proj_kept, 16)
            stage(0, 0, 0)
            stage(0, 0, 1)
            for qb in range(TT):
                with pool.Fori(0, HEADS // 2 - 1) as i:
                    for u in range(2):
                        g = 16 * qb + 2 * i + u
                        mask(qb, g, u)
                        stage(qb, i + 1, u)
                if qb:
                    pool.wait_ge(x_made, qb)
                pool.dma_start(bcB[:, :], x[qb * P:(qb + 1) * P, :]).then_inc(x_again, 16)
                for u in range(2):
                    mask(qb, 16 * qb + 14 + u, u)
                    if qb < TT - 1:
                        stage(qb + 1, 0, u)

            def moe(l):
                pool.wait_ge(stored[l], 16)
                pool.wait_ge(dest_made[l], 1)
                for k in range(2):
                    for t in range(TT):
                        pool.indirect_dma_start(
                            out=tok_dram[l], out_offset=bass.IndirectOffsetOnAxis(ap=dest[:, k, t:t + 1], axis=0),
                            in_=tokid[:, t:t + 1], in_offset=None).then_inc(table_filled[l], 16)
                pool.wait_ge(table_filled[l], 16 * 2 * TT)
                pool.dma_start(slot_row[:, :], tok_dram[l].rearrange("(b p) a -> b (p a)", p=P)).then_inc(
                    table_read[l], 16)
                pool.wait_ge(table_made[l], 1)
                for b in range(2):
                    pool.wait_ge(h_stored[b], 16 * TT // 2 * (l + 1))

                def gather(b):
                    nc.gpsimd.tensor_copy(idx_now[:, :], slot_tok[:, ds(b, 1)])
                    pool.drain()
                    pool.indirect_dma_start(
                        out=xg, out_offset=None, in_=h_dram[l],
                        in_offset=bass.IndirectOffsetOnAxis(ap=idx_now[:, 0:1], axis=0)).then_inc(x_gathered[l], 16)

                gather(0)
                pool.wait_ge(x_turned[l], 1)
                gather(1)
                blocks = pool.value_load(bounds[0:1, E:E + 1], min_val=1, max_val=MAXBLK)
                with pool.Fori(0, blocks) as b:
                    pool.wait_ge(x_turned[l], b + 2)
                    gather(b + 2)
                    pool.wait_ge(y_kept[l], 2 * b + 2)
                    pool.dma_start(y_dram[l][ds(b * P, P), :], yo).then_inc(stored[l], 16)
                    pool.wait_ge(x_gathered[l], 16 * b + 48)
                    pool.wait_ge(stored[l], 16 * b + 32)
                for t in range(TT):
                    if t >= 2:
                        pool.wait_ge(x_added[l], t - 1)
                    for k in range(2):
                        pool.indirect_dma_start(
                            out=ygat[:, t % 2, k, :], out_offset=None, in_=y_dram[l],
                            in_offset=bass.IndirectOffsetOnAxis(ap=dest[:, k, t:t + 1], axis=0)
                        ).then_inc(y_gathered[l][t % 2], 16)

            norm(1, lambda: pool.wait_ge(x_made, TT))
            moe(0)
            norm(2, lambda: pool.wait_ge(x_added[0], TT))
            pool.wait_ge(h_made, TT * 3)
            pool.dma_start(bcA[:, :], b_out.partition_broadcast(P)).then_inc(bout_loaded, 16)
            for c in range(DC):
                for j in range(1, ADD_TAPS):
                    pool.wait_ge(tap_made, c * ADD_TAPS + j + 1)
                    nc.gpsimd.tensor_tensor(acc2, acc2, tapp[:, j % 2, :], ALU.add).then_inc(tap_added, 1)
                    if j < ADD_TAPS - 1:
                        pool.wait_ge(tap_added, c * (ADD_TAPS - 1) + j)
            norm(3, lambda: pool.wait_ge(out_used, 2 * TT))
            moe(1)
            pool.wait_ge(x_added[1], TT)
            pool.dma_start(bcA[:, :], norm_g[4].partition_broadcast(P)).then_inc(bc_loaded, 16)

        @block.scalar
        def _(act):
            act.wait_ge(cols_loaded, 64)
            nc.scalar.activation(cond[:, :], ccol, ACT.Silu).then_inc(cond_made, 1)

            def norm_stats(n, free):
                free()
                for t in range(TT):
                    if n and t == 0:
                        act.wait_ge(h_kept, TT * n)
                    nc.scalar.activation(oT[:, :, :].rearrange("p c t -> p (c t)"),
                                         xq[:, t, :, :].rearrange("p c j -> p (c j)"), ACT.Square,
                                         accum_out=ss[:, t:t + 1]).then_inc(sq_done, 1)
                    act.wait_ge(sq_done, TT * n + t + 1)
                act.wait_ge(ms_done, n + 1)
                nc.scalar.activation(rstd[:, :], ss[:, :], ACT.Sqrt).then_inc(root_done, 1)

            def norm_keep(n):
                for t in range(TT):
                    act.wait_ge(h_turned, TT * n + t + 1)
                    nc.scalar.activation(hT[:, :, t * P:(t + 1) * P],
                                         bank(2 * (t % 2), 2).rearrange("p (c t) -> p c t", c=DC),
                                         ACT.Copy).then_inc(h_kept, 1)

            norm_stats(0, lambda: act.wait_ge(x_loaded, 16))
            norm_keep(0)
            for cc in range(16):
                act.wait_ge(proj_done, cc + 1)
                src = bank(2 * (cc % 2), 2)
                if cc < 8:
                    nc.scalar.activation(xq[:, :, cc, :], src.rearrange("p (t j) -> p t j", t=TT),
                                         ACT.Copy).then_inc(proj_kept, 1)
                else:
                    nc.scalar.activation(kT[:, cc - 8, :], src, ACT.Copy).then_inc(proj_kept, 1)
            act.wait_ge(zeros_stored, 32)
            for t in range(TT):
                act.wait_ge(proj_done, 16 + 2 * (t + 1))
                nc.scalar.activation(vt[:, t, :], bank(2 * (t % 2), 2), ACT.Copy).then_inc(proj_kept, 1)

            def sigmoids(qb, g, u, early=False):
                w = (qb + 1) * P
                act.wait_ge(z_done, g + 1)
                if not early:
                    act.wait_ge(prob_made, g - 1)
                nc.scalar.activation(beta[:, u, 0:w], bank(2 * u, 2)[:, 0:w], ACT.Sigmoid, scale=HD ** -0.5)
                nc.scalar.activation(omega[:, u, 0:w], bank(2 * u, 2)[:, 0:w], ACT.Sigmoid,
                                     scale=-HD ** -0.5).then_inc(sig_done, 1)

            def keep_turned(qb, g, u):
                w = (qb + 1) * P
                act.wait_ge(prob_turned, g + 1)
                nc.scalar.activation(probT[:, u, 0:w], bank(4, 2)[:, 0:w], ACT.Copy).then_inc(probT_kept, 1)

            sigmoids(0, 0, 0, early=True)
            sigmoids(0, 1, 1, early=True)
            for qb in range(TT):
                with act.Fori(0, HEADS // 2 - 1) as i:
                    for u in range(2):
                        g = 16 * qb + 2 * i + u
                        sigmoids(qb, g + 2, u)
                        keep_turned(qb, g, u)
                for u in range(2):
                    g = 16 * qb + 14 + u
                    if qb < TT - 1:
                        sigmoids(qb + 1, g + 2, u)
                    keep_turned(qb, g, u)
                for half in range(2):
                    act.wait_ge(o_turned, 2 * qb + half + 1)
                    nc.scalar.activation(oT[:, 4 * half:4 * half + 4, :],
                                         bank(7).rearrange("p (c t) -> p c t", c=4), ACT.Copy).then_inc(oT_kept, 1)

            def moe(l):
                act.wait_ge(logits_done[l], 1)
                nc.scalar.activation(tmp(0), bank(4)[:, 0:TT * E].rearrange("p (t e) -> p t e", t=TT),
                                     ACT.Sigmoid).then_inc(score_done[l], 1)

                def keep(b):
                    act.wait_ge(x_turned[l], b + 1)
                    nc.scalar.activation(xT, bank(2, 2).rearrange("p (c t) -> p c t", c=DC), ACT.Copy).then_inc(
                        xT_kept[l], 1)

                keep(0)
                blocks = act.value_load(bounds[0:1, E:E + 1], min_val=1, max_val=MAXBLK)
                with act.Fori(0, blocks) as b:
                    act.wait_ge(gate_done[l], b + 1)
                    nc.scalar.activation(sg, bank(0), ACT.Silu).then_inc(silu_done[l], 1)
                    act.wait_ge(up_done[l], b + 1)
                    keep(b + 1)

            norm_stats(1, lambda: act.wait_ge(x_made, TT))
            norm_keep(1)
            moe(0)
            norm_stats(2, lambda: act.wait_ge(x_added[0], TT))
            norm_keep(2)
            for c in range(DC):
                g = 4 * (c % 2)
                act.wait_ge(in_done, c + 1)
                nc.scalar.activation(usig[:, c % 2, :], bank(g + 2, 2), ACT.Sigmoid,
                                     bias=b_in_c[:, 8 + c:9 + c]).then_inc(usig_done, 1)
                act.wait_ge(u_done, c + 1)
                for j in range(ADD_TAPS):
                    if j == 0:
                        if c:
                            act.wait_ge(conv_done, c)
                        dst = acc2
                    else:
                        if c or j > 2:
                            act.wait_ge(tap_added, c * (ADD_TAPS - 1) + max(j - 2, 0))
                        dst = tapp[:, j % 2, :]
                    nc.scalar.activation(dst, upad[:, c % 2, j:j + T], ACT.Copy,
                                         scale=w_dw_c[:, c, j:j + 1]).then_inc(tap_made, 1)
            for c in range(DC):
                act.wait_ge(centered, c + 1)
                if c >= 2:
                    act.wait_ge(var_done, c - 1)
                nc.scalar.activation(usig[:, c % 2, :], cv[:, c, :], ACT.Square).then_inc(squared, 1)
            act.wait_ge(ln_root, 1)
            nc.scalar.activation(tapp[:, 0, :], tapp[:, 1, :], ACT.Sqrt).then_inc(ln_root, 1)
            for c in range(DC):
                act.wait_ge(ln_scaled, c + 1)
                nc.scalar.activation(hT[:, c, :], cv[:, c, :], ACT.Silu, bias=ln_b_c[:, c:c + 1],
                                     scale=ln_g_c[:, c:c + 1]).then_inc(ln_done, 1)
            norm_stats(3, lambda: act.wait_ge(out_used, 2 * TT))
            norm_keep(3)
            moe(1)
            norm_stats(4, lambda: act.wait_ge(x_added[1], TT))

        @block.vector
        def _(dve):
            steps = [0]

            def step(ins):
                steps[0] += 1
                ins.then_inc(dve_step, 1)
                dve.wait_ge(dve_step, steps[0])

            V = nc.vector
            V.memset(spare[:, 0:D], 0.0).then_inc(zeros_made, 1)
            for n, dst in enumerate((tokid[:, :], pref_g[:, :, :].rearrange("p t g -> p (t g)"),
                                     pref_e[:, :, :].rearrange("p t e -> p (t e)"))):
                dve.wait_ge(const_made, 3 + n)
                step(V.tensor_copy(dst, iota_i[:, 0:dst.shape[1]]))
            dve.wait_ge(cols_loaded, 64)
            with dve.Fori(0, 2 * ADA // 3) as i:
                for k in range(3):
                    dve.wait_ge(ada_used, 3 * i + k + 1)
                    at = kv[0:1, ds(i * 1536 + 512 * k, 512)]
                    V.tensor_tensor(at, bank(k)[0:1, :], at, ALU.add).then_inc(ada_row, 1)

            def norm(n):
                dve.wait_ge(sq_done, TT * (n + 1))
                V.tensor_scalar(ss[:, :], ss[:, :], 1.0 / D, EPS, ALU.mult, ALU.add).then_inc(ms_done, 1)
                dve.wait_ge(root_done, n + 1)
                V.reciprocal(rstd[:, :], rstd[:, :]).then_inc(rstd_done, 1)
                dve.wait_ge(bc_loaded, 48 * (n + 1) if n < 4 else 48 * 4 + 16)
                if n < 4:
                    V.scalar_tensor_tensor(bcA[:, :], bcA[:, :], 1.0, bcC[:, :], ALU.add, ALU.mult).then_inc(a_made, 1)
                    dve.wait_ge(a_made, n + 1)
                dve.wait_ge(rstd_done, n + 1)
                for t in range(TT):
                    if n < 4:
                        if t >= 2:
                            dve.wait_ge(h_turned, TT * n + t - 1)
                        if n % 2 and t >= 2:
                            dve.wait_ge(h_stored[t % 2], 16 * (TT // 2 * (n // 2) + t // 2))
                    elif t >= 2:
                        dve.wait_ge(out_stored[t % 2], 16 * (t // 2))
                    h = pbuf[:, t % 2, 0:D]
                    ins = V.scalar_tensor_tensor(h, xq[:, t, :, :].rearrange("p c j -> p (c j)"), rstd[:, t:t + 1],
                                                 bcA[:, :], ALU.mult, ALU.mult)
                    if n < 4:
                        ins.then_inc(h_scaled, 1)
                        dve.wait_ge(h_scaled, TT * n + t + 1)
                        V.tensor_tensor(h, h, bcB[:, :], ALU.add).then_inc(h_made, 1)
                    else:
                        ins.then_inc(final_made, 1)

            norm(0)

            def probabilities(qb, g, u, early=False):
                w = (qb + 1) * P
                dve.wait_ge(masked, g + 1)
                V.tensor_tensor_scan(pbuf[:, u, D - w:D][:, ::-1], omega[:, u, 0:w][:, ::-1], omega[:, u, 0:w], 1.0,
                                     ALU.mult, ALU.bypass).then_inc(scanned, 1)
                dve.wait_ge(scanned, g + 1)
                if not early:
                    dve.wait_ge(prob_turned, g - 1)
                V.tensor_tensor(prob[:, u, 0:w], beta[:, u, 0:w], pbuf[:, u, D - w + 1:D + 1],
                                ALU.mult).then_inc(prob_made, 1)

            def keep_o(pair, chunk):
                dve.wait_ge(av_done, 2 * pair + 2)
                V.tensor_copy(bcA[:, ds(chunk * P, P)], bank(6)[:, 0:P]).then_inc(o_kept, 1)

            def add_projection(qb):
                dve.wait_ge(wo_done, qb + 1)
                dve.wait_ge(gate_loaded, 16)
                dve.wait_ge(x_again, 16 * (qb + 1))
                V.tensor_tensor(bcA[:, :], bank(4, 2), bcC[:, :], ALU.mult).then_inc(wo_scaled, 1)
                dve.wait_ge(wo_scaled, qb + 1)
                V.tensor_tensor(xq[:, qb, :, :].rearrange("p c j -> p (c j)"), bcA[:, :], bcB[:, :],
                                ALU.add).then_inc(x_made, 1)

            for qb in range(TT):
                for u in range(2):
                    probabilities(qb, 16 * qb + u, u, early=(qb == 0))
                if qb:
                    add_projection(qb - 1)
                with dve.Fori(1, HEADS // 2) as i:
                    for u in range(2):
                        probabilities(qb, 16 * qb + 2 * i + u, u)
                    keep_o(8 * qb + i - 1, i - 1)
                keep_o(8 * qb + 7, 7)
            add_projection(TT - 1)

            def moe(l):
                sc, sel, a, b, m0, m1, both_ = (tmp(n) for n in (0, 1, 2, 3, 4, 5, 6))
                gs, g1, g2, g3 = (tmp(n, GROUPS) for n in (7, 8, 9, 10))
                one = lambda n: tmp(n, 1)

                def wide(ap, w):
                    return ap.to_broadcast([P, TT, w])

                dve.wait_ge(score_done[l], 1)
                dve.wait_ge(cols_loaded, 64)
                step(V.tensor_tensor(sel, sc, brt[:, :].unsqueeze(1).to_broadcast([P, TT, E]), ALU.add))
                s4 = sel.rearrange("p t (g e) -> p t g e", e=EPG)
                r = [s4[:, :, :, j] for j in range(EPG)]
                V.tensor_tensor(gs, r[0], r[1], ALU.max)
                V.tensor_tensor(g1, r[0], r[1], ALU.min)
                V.tensor_tensor(g2, r[2], r[3], ALU.max)
                step(V.tensor_tensor(g3, r[2], r[3], ALU.min))
                step(V.tensor_tensor(g1, g1, g3, ALU.max))
                step(V.tensor_tensor(g3, gs, g2, ALU.min))
                step(V.tensor_tensor(gs, gs, g2, ALU.max))
                step(V.tensor_tensor(g1, g1, g3, ALU.max))
                step(V.tensor_tensor(gs, gs, g1, ALU.add))

                def first_largest(dst, src, prefer, w, scratch, top):
                    step(V.tensor_reduce(top, src, AX.X, ALU.max))
                    step(V.tensor_tensor(scratch, src, wide(top, w), ALU.is_equal))
                    step(V.tensor_tensor(scratch, scratch, prefer, ALU.mult))
                    step(V.tensor_reduce(top, scratch, AX.X, ALU.max))
                    step(V.tensor_tensor(dst, scratch, wide(top, w), ALU.is_equal))

                first_largest(g2, gs, pref_g[:, :, :], GROUPS, g1, one(11))
                step(V.tensor_scalar(g3, g2, -1.0, 1e30, ALU.add, ALU.mult))
                a4, w4 = a.rearrange("p t (g e) -> p t g e", e=EPG), [P, TT, GROUPS, EPG]
                for j in range(EPG):
                    V.tensor_tensor(a4[:, :, :, j], r[j], g2, ALU.mult)
                step(V.memset(both_, 0.0))
                for j in range(EPG):
                    ins = V.tensor_tensor(a4[:, :, :, j], a4[:, :, :, j], g3, ALU.add)
                step(ins)
                first_largest(m0, a, pref_e[:, :, :], E, b, one(11))
                step(V.tensor_scalar(b, m0, -1e30, None, ALU.mult))
                step(V.tensor_tensor(a, a, b, ALU.add))
                first_largest(m1, a, pref_e[:, :, :], E, b, one(11))
                step(V.tensor_tensor(both_, m0, m1, ALU.add))
                run = spare[:, 12 * P:12 * P + (TT + 1) * E].rearrange("p (t e) -> p t e", e=E)
                step(V.memset(run[:, 0, :], 0.0))
                for t in range(TT):
                    step(V.tensor_tensor(run[:, t + 1, :], run[:, t, :], both_[:, t, :], ALU.add))
                V.tensor_copy(b, both_).then_inc(picked[l], 1)
                for k, m in enumerate((m0, m1)):
                    step(V.tensor_tensor(a, sc, m, ALU.mult))
                    step(V.tensor_reduce(wts[:, k, :], a, AX.X, ALU.add))
                step(V.tensor_tensor(one(11)[:, :, 0], wts[:, 0, :], wts[:, 1, :], ALU.add))
                step(V.reciprocal(one(11)[:, :, 0], one(11)[:, :, 0]))
                for k in range(2):
                    step(V.tensor_tensor(wts[:, k, :], wts[:, k, :], one(11)[:, :, 0], ALU.mult))
                dve.wait_ge(counted[l], 1)
                cnt, nb, cum, zero = (spare[:, (14 + n) * P:(14 + n) * P + E] for n in range(4))
                step(V.memset(nb, 1.0))
                step(V.memset(zero, 0.0))
                step(V.tensor_copy(cnt, bank(5)[:, P:P + E]))
                for j in range(1, T // P):
                    step(V.scalar_tensor_tensor(nb, cnt, float(j * P), nb, ALU.is_gt, ALU.add))
                step(V.tensor_tensor_scan(cum, nb, zero, 0.0, ALU.add, ALU.add))
                V.memset(bounds[:, :], 0)
                V.tensor_tensor(nb, cum, nb, ALU.subtract).then_inc(dve_step, 1)
                steps[0] += 1
                dve.wait_ge(dve_step, steps[0])
                V.tensor_copy(bounds[:, 1:E + 1], cum[0:1, :]).then_inc(bounds_made[l], 1)
                step(V.tensor_scalar(nb, nb, float(P), None, ALU.mult))
                step(V.tensor_tensor(b, bank(5)[:, 0:P].rearrange("p (t e) -> p t e", t=TT),
                                     nb.unsqueeze(1).to_broadcast([P, TT, E]), ALU.add))
                for k, m in enumerate((m0, m1)):
                    step(V.tensor_tensor(a, b, m, ALU.mult))
                    step(V.tensor_reduce(one(11)[:, :, 0], a, AX.X, ALU.add))
                    step(V.tensor_copy(dest[:, k, :], one(11)[:, :, 0]))
                V.tensor_copy(cnt, nb).then_inc(dest_made[l], 1)
                dve.wait_ge(table_turned[l], 1)
                V.tensor_copy(slot_tok[:, :], bank(6)[:, 0:TABLE]).then_inc(table_made[l], 1)

                blocks = dve.value_load(bounds[0:1, E:E + 1], min_val=1, max_val=MAXBLK)
                with dve.Fori(0, blocks) as n:
                    dve.wait_ge(silu_done[l], n + 1)
                    dve.wait_ge(up_done[l], n + 1)
                    for f in range(2):
                        at = slice(256 * f, 256 * f + 256)
                        V.tensor_tensor(ha[:, at], sg[:, at], bank(1)[:, at], ALU.mult).then_inc(ha_made[l], 1)
                    dve.wait_ge(ha_turned[l], n + 1)
                    V.tensor_copy(haT, bank(4)).then_inc(haT_kept[l], 1)
                    dve.wait_ge(stored[l], 16 * n + 16)
                    for f in range(2):
                        dve.wait_ge(down_done[l], 2 * n + f + 1)
                        V.tensor_copy(yo[:, 512 * f:512 * f + 512], bank(5 + f)).then_inc(y_kept[l], 1)
                dve.wait_ge(gate_loaded, 16 * (2 * l + 2))
                for t in range(TT):
                    dve.wait_ge(y_gathered[l][t % 2], 32 * (t // 2 + 1))
                    y0, y1 = ygat[:, t % 2, 0, :], ygat[:, t % 2, 1, :]
                    xt = xq[:, t, :, :].rearrange("p c j -> p (c j)")
                    step(V.tensor_scalar(y0, y0, wts[:, 0, t:t + 1], None, ALU.mult))
                    step(V.scalar_tensor_tensor(y0, y1, wts[:, 1, t:t + 1], y0, ALU.mult, ALU.add))
                    step(V.tensor_tensor(y0, y0, bcC[:, :], ALU.mult))
                    V.tensor_tensor(xt, xt, y0, ALU.add).then_inc(x_added[l], 1)

            norm(1)
            moe(0)
            norm(2)
            step(V.memset(upad[:, :, 0:CW - 1], 0.0))
            for c in range(DC):
                g = 4 * (c % 2)
                dve.wait_ge(usig_done, c + 1)
                u = upad[:, c % 2, :]
                V.scalar_tensor_tensor(u[:, CW - 1:UW], bank(g, 2), b_in_c[:, c:c + 1], usig[:, c % 2, :], ALU.add,
                                       ALU.mult).then_inc(u_done, 1)
                dve.wait_ge(u_done, c + 1)
                step(V.tensor_scalar(cv[:, c, :], u[:, ADD_TAPS:ADD_TAPS + T], w_dw_c[:, c, ADD_TAPS:ADD_TAPS + 1],
                                     b_dw_c[:, c:c + 1], ALU.mult, ALU.add))
                for k in range(ADD_TAPS + 1, CW):
                    step(V.scalar_tensor_tensor(cv[:, c, :], u[:, k:k + T], w_dw_c[:, c, k:k + 1], cv[:, c, :],
                                                ALU.mult, ALU.add))
                dve.wait_ge(tap_added, (c + 1) * (ADD_TAPS - 1))
                V.tensor_tensor(cv[:, c, :], cv[:, c, :], acc2, ALU.add).then_inc(conv_done, 1)
            dve.wait_ge(mean_done, 1)
            step(V.tensor_scalar(usig[:, 0, :], bank(0, 2), 1.0 / D, None, ALU.mult))
            step(V.tensor_copy(acc2, usig[:, 0, :]))
            for c in range(DC):
                V.tensor_tensor(cv[:, c, :], cv[:, c, :], acc2, ALU.subtract).then_inc(centered, 1)
            dve.wait_ge(var_done, DC)
            V.tensor_scalar(tapp[:, 1, :], bank(2, 2), 1.0 / D, EPS, ALU.mult, ALU.add).then_inc(ln_root, 1)
            dve.wait_ge(ln_root, 2)
            step(V.reciprocal(tapp[:, 0, :], tapp[:, 0, :]))
            for c in range(DC):
                V.tensor_tensor(cv[:, c, :], cv[:, c, :], tapp[:, 0, :], ALU.mult).then_inc(ln_scaled, 1)
            dve.wait_ge(bout_loaded, 16)
            dve.wait_ge(gate_loaded, 16 * 3)
            for t in range(TT):
                for half in range(2):
                    n = 2 * t + half
                    cs = slice(512 * half, 512 * half + 512)
                    dve.wait_ge(out_done, n + 1)
                    y = acc2[:, cs]
                    step(V.tensor_tensor(y, bank(4 + n % 4), bcA[:, cs], ALU.add))
                    step(V.tensor_tensor(y, y, bcC[:, cs], ALU.mult))
                    xt = xq[:, t, 4 * half:4 * half + 4, :].rearrange("p c j -> p (c j)")
                    V.tensor_tensor(xt, xt, y, ALU.add).then_inc(out_used, 1)
            norm(3)
            moe(1)
            norm(4)

        @block.tensor
        def _(pe):
            mm = nc.tensor.matmul
            pe.wait_ge(cond_made, 1)
            with pe.Fori(0, 2 * ADA // 3) as i:
                for k in range(3):
                    pe.wait_ge(slot_loaded[k], 16 * i + 16)
                    for c in range(DC):
                        ins = mm(bank(k)[0:1, :], cond[:, c:c + 1], ring[:, k, 512 * c:512 * c + 512],
                                 start=(c == 0), stop=(c == DC - 1))
                    ins.then_inc(ada_used, 1)
                    if k == 2:
                        pe.wait_ge(ada_row, 3 * i + 3)
            pe.wait_ge(const_made, 2)

            def norm(n):
                for t in range(TT):
                    pe.wait_ge(h_made, TT * n + t + 1)
                    if t >= 2:
                        pe.wait_ge(h_kept, TT * n + t - 1)
                    for c in range(DC):
                        ins = nc.tensor.transpose(bank(2 * (t % 2), 2)[:, c * P:(c + 1) * P],
                                                  pbuf[:, t % 2, c * P:(c + 1) * P], ident[:, :])
                    ins.then_inc(h_turned, 1)
                pe.wait_ge(h_kept, TT * (n + 1))

            norm(0)
            for cc in range(16):
                j, q = cc // 4, cc % 4
                if q == 0:
                    pe.wait_ge(at_loaded[j], 16)
                if cc >= 2:
                    pe.wait_ge(proj_kept, cc - 1)
                for half in range(2):
                    for c in range(DC):
                        ins = mm(bank(2 * (cc % 2) + half), ring[:, j % 3, 512 * c + P * q:512 * c + P * q + P],
                                 hT[:, c, 512 * half:512 * half + 512], start=(c == 0), stop=(c == DC - 1))
                ins.then_inc(proj_done, 1)
            for t in range(TT):
                if t == 0:
                    pe.wait_ge(at_loaded[4], 16)
                    pe.wait_ge(at_loaded[5], 16)
                pe.wait_ge(proj_kept, 15 + t)
                for half in range(2):
                    for c in range(DC):
                        ins = mm(bank(2 * (t % 2) + half), hT[:, c, t * P:(t + 1) * P],
                                 ring[:, (4 + half) % 3, 512 * c:512 * c + 512], start=(c == 0), stop=(c == DC - 1))
                    ins.then_inc(proj_done, 1)

            def scores(qb, g, u, chunk, early=False):
                w = (qb + 1) * P
                pe.wait_ge(q_staged, g + 1)
                if not early:
                    pe.wait_ge(sig_done, g - 1)
                for n0 in range(0, w, 512):
                    n1 = min(w, n0 + 512)
                    ins = mm(bank(2 * u, 2)[:, n0:n1], qstage[:, u, :],
                             kT[:, ds(chunk, 1), n0:n1].rearrange("p a t -> p (a t)"), start=True, stop=True)
                ins.then_inc(z_done, 1)

            def turn_probabilities(qb, g, u, first=False):
                pe.wait_ge(prob_made, g + 1)
                if first and qb:
                    pe.wait_ge(wo_scaled, qb)
                if not first or qb:
                    pe.wait_ge(probT_kept, g)
                for s in range(qb + 1):
                    ins = nc.tensor.transpose(bank(4, 2)[:, s * P:(s + 1) * P], prob[:, u, s * P:(s + 1) * P],
                                              ident[:, :])
                ins.then_inc(prob_turned, 1)

            def values(qb, g, u, chunk, pair):
                pe.wait_ge(probT_kept, g + 1)
                if u == 0 and pair is not None:
                    pe.wait_ge(o_kept, pair)
                for s in range(qb + 1):
                    ins = mm(bank(6)[:, HD * u:HD * u + HD], probT[:, u, s * P:(s + 1) * P],
                             vt[:, s, ds(chunk * P + HD * u, HD)], start=(s == 0), stop=(s == qb))
                ins.then_inc(av_done, 1)

            pe.wait_ge(proj_kept, 24)
            scores(0, 0, 0, 0, early=True)
            scores(0, 1, 1, 0, early=True)
            for qb in range(TT):
                last = qb == TT - 1
                g = 16 * qb
                scores(qb, g + 2, 0, 1)
                turn_probabilities(qb, g, 0, first=True)
                scores(qb, g + 3, 1, 1)
                turn_probabilities(qb, g + 1, 1)
                values(qb, g, 0, 0, 8 * qb if qb else None)
                with pe.Fori(1, HEADS // 2 - 1) as i:
                    gi = g + 2 * i
                    scores(qb, gi + 2, 0, i + 1)
                    turn_probabilities(qb, gi, 0)
                    values(qb, gi - 1, 1, i - 1, None)
                    scores(qb, gi + 3, 1, i + 1)
                    turn_probabilities(qb, gi + 1, 1)
                    values(qb, gi, 0, i, 8 * qb + i)
                if not last:
                    scores(qb + 1, g + 16, 0, 0)
                turn_probabilities(qb, g + 14, 0)
                values(qb, g + 13, 1, 6, None)
                if not last:
                    scores(qb + 1, g + 17, 1, 0)
                turn_probabilities(qb, g + 15, 1)
                values(qb, g + 14, 0, 7, 8 * qb + 7)
                values(qb, g + 15, 1, 7, None)
                pe.wait_ge(o_kept, 8 * qb + 8)
                if qb == 0:
                    pe.wait_ge(at_loaded[6], 16)
                    pe.wait_ge(at_loaded[7], 16)
                for half in range(2):
                    pe.wait_ge(oT_kept, 2 * qb + half) if 2 * qb + half else None
                    for c in range(4):
                        ins = nc.tensor.transpose(bank(7)[:, c * P:(c + 1) * P],
                                                  bcA[:, (4 * half + c) * P:(4 * half + c + 1) * P], ident[:, :])
                    ins.then_inc(o_turned, 1)
                pe.wait_ge(oT_kept, 2 * qb + 2)
                for half in range(2):
                    for c in range(DC):
                        ins = mm(bank(4 + half), oT[:, c, :], ring[:, half, 512 * c:512 * c + 512],
                                 start=(c == 0), stop=(c == DC - 1))
                ins.then_inc(wo_done, 1)

            def moe(l):
                for t in range(TT):
                    for c in range(DC):
                        ins = mm(bank(4)[:, E * t:E * t + E], hT[:, c, t * P:(t + 1) * P], wr[:, c, :],
                                 start=(c == 0), stop=(c == DC - 1))
                ins.then_inc(logits_done[l], 1)
                pe.wait_ge(picked[l], 1)
                run = spare[:, 12 * P:12 * P + (TT + 1) * E]
                mm(bank(5)[:, 0:P], upper[:, :], spare[:, 6 * P:7 * P], start=True, stop=False)
                mm(bank(5)[:, 0:P], ones[:, :], run[:, 0:P], start=False, stop=True)
                mm(bank(5)[:, P:P + E], ones[:, :], run[:, P:P + E], start=True, stop=True).then_inc(counted[l], 1)
                pe.wait_ge(table_read[l], 16)
                nc.tensor.transpose(bank(6)[:, 0:TABLE], slot_row[:, :], ident[0:TABLE, 0:TABLE]).then_inc(
                    table_turned[l], 1)

                def turn_rows(b):
                    pe.wait_ge(x_gathered[l], 16 * b + 16)
                    for c in range(DC):
                        ins = nc.tensor.transpose(bank(2, 2)[:, c * P:(c + 1) * P], xg[:, c * P:(c + 1) * P],
                                                  ident[:, :])
                    ins.then_inc(x_turned[l], 1)

                turn_rows(0)
                with pe.Fori(0, E // 2) as i:
                    for s in range(2):
                        wg, wu, wd = wset[s]
                        first = pe.value_load(bounds[0:1, ds(2 * i + s, 1)], min_val=0, max_val=MAXBLK)
                        end = pe.value_load(bounds[0:1, ds(2 * i + s + 1, 1)], min_val=1, max_val=MAXBLK)
                        with pe.Fori(first, end) as b:
                            pe.wait_ge(xT_kept[l], b + 1)
                            for w, at, done in ((wg, 0, gate_done), (wu, 1, up_done)):
                                pe.wait_ge(w_loaded[l][s][at], 16 * i + 16)
                                for c in range(DC):
                                    ins = mm(bank(at), xT[:, c, :], w[:, F * c:F * c + F],
                                             start=(c == 0), stop=(c == DC - 1))
                                ins.then_inc(done[l], 1)
                            turn_rows(b + 1)
                            for f in range(2):
                                pe.wait_ge(ha_made[l], 2 * b + f + 1)
                                for c in (2 * f, 2 * f + 1):
                                    ins = nc.tensor.transpose(bank(4)[:, c * P:(c + 1) * P], ha[:, c * P:(c + 1) * P],
                                                              ident[:, :])
                            ins.then_inc(ha_turned[l], 1)
                            pe.wait_ge(w_loaded[l][s][2], 16 * i + 16)
                            pe.wait_ge(haT_kept[l], b + 1)
                            for half in range(2):
                                for c in range(F // P):
                                    ins = mm(bank(5 + half), haT[:, c * P:(c + 1) * P],
                                             wd[:, D * c + 512 * half:D * c + 512 * half + 512],
                                             start=(c == 0), stop=(c == F // P - 1))
                                ins.then_inc(down_done[l], 1)

            norm(1)
            moe(0)
            norm(2)
            for c in range(DC):
                g = 4 * (c % 2)
                if c % 4 == 0:
                    pe.wait_ge(cv_loaded[c // 2], 16)
                    pe.wait_ge(cv_loaded[c // 2 + 1], 16)
                if c >= 2:
                    pe.wait_ge(u_done, c - 1)
                for part in range(2):
                    slot = (2 * (c // 4) + part) % 3
                    for half in range(2):
                        for k in range(DC):
                            ins = mm(bank(g + 2 * part + half),
                                     ring[:, slot, 512 * k + P * (c % 4):512 * k + P * (c % 4) + P],
                                     hT[:, k, 512 * half:512 * half + 512], start=(k == 0), stop=(k == DC - 1))
                ins.then_inc(in_done, 1)
            pe.wait_ge(u_done, DC)
            for c in range(DC):
                pe.wait_ge(conv_done, c + 1)
                for half in range(2):
                    ins = mm(bank(half), ones[:, :], cv[:, c, 512 * half:512 * half + 512],
                             start=(c == 0), stop=(c == DC - 1), skip_group_check=True)
            ins.then_inc(mean_done, 1)
            for c in range(DC):
                pe.wait_ge(squared, c + 1)
                for half in range(2):
                    ins = mm(bank(2 + half), ones[:, :], usig[:, c % 2, 512 * half:512 * half + 512],
                             start=(c == 0), stop=(c == DC - 1), skip_group_check=True)
                ins.then_inc(var_done, 1)
            pe.wait_ge(ln_done, DC)
            pe.wait_ge(cv_loaded[4], 16)
            pe.wait_ge(cv_loaded[5], 16)
            for t in range(TT):
                for half in range(2):
                    n = 2 * t + half
                    if n >= 4:
                        pe.wait_ge(out_used, n - 3)
                    for c in range(DC):
                        ins = mm(bank(4 + n % 4), hT[:, c, t * P:(t + 1) * P],
                                 ring[:, (4 + half) % 3, 512 * c:512 * c + 512], start=(c == 0), stop=(c == DC - 1))
                    ins.then_inc(out_done, 1)
            norm(3)
            moe(1)


def kernel(**inputs):
    import numpy as np
    import concourse.bacc as bacc
    from concourse.bass_utils import run_bass_kernel_spmd

    a = {k: np.asarray(v) for k, v in inputs.items()}

    def pieces(w, k, order=None):
        w = w.reshape(-1, k, P, w.shape[-1] // 512, 512).transpose(0, 3, 2, 1, 4)
        w = w.reshape(-1, P, k * 512)
        return np.ascontiguousarray(w if order is None else w[order])

    def col(v):
        return v.reshape(-1, P).T

    def rows(w, k):
        return np.ascontiguousarray(w.reshape(-1, k, P, w.shape[-1]).transpose(0, 2, 1, 3)).reshape(-1, P, k * w.shape[-1])

    zeros = np.zeros((P, 8), np.float32)
    dw = a["cv_w_dw"][0].reshape(CW, DC, P).transpose(2, 1, 0).reshape(P, DC * CW)
    data = {
        "x": a["x"].reshape(T, D),
        "c_col": col(a["c"]),
        "b_ada": a["b_ada"].reshape(1, -1),
        "norm_g": np.stack([a["norm1_g"][0], a["norm2_g"][0], a["norm1_g"][1], a["norm2_g"][1], a["final_g"]]),
        "vec_cols": np.concatenate([col(a["c"]), col(a["cv_b_in"]), dw, col(a["cv_b_dw"]), col(a["cv_ln_g"]),
                                    col(a["cv_ln_b"]), zeros], axis=1),
        "b_out": a["cv_b_out"].reshape(D),
        "b_router": a["b_router"],
        "w_router": a["w_router"].reshape(DC, P, E).transpose(1, 0, 2),
        "w_ada": pieces(a["w_ada"], DC),
        "w_qkv": pieces(a["sb_w_qkv"], DC),
        "w_o": pieces(a["sb_w_o"], DC),
        "w_in": pieces(a["cv_w_in"], DC, [0, 2, 1, 3]),
        "w_out": pieces(a["cv_w_out"], DC),
        "w_gate": rows(a["moe_w_gate"], DC),
        "w_up": rows(a["moe_w_up"], DC),
        "w_down": rows(a["moe_w_down"], F // P),
    }
    nc = bacc.Bacc("TRN2", target_bir_lowering=False, num_devices=1)
    arrays, args = {}, []
    for name, v in data.items():
        v = np.ascontiguousarray(v)
        arrays[f"in_{name}"] = v
        args.append(nc.dram_tensor(f"in_{name}", v.shape, mybir.dt.from_np(v.dtype), kind="ExternalInput").ap())
    out = nc.dram_tensor("out_x", (T, D), mybir.dt.float32, kind="ExternalOutput").ap()
    trunk(nc, *args, out)
    r = run_bass_kernel_spmd(nc, [arrays], core_ids=[0])
    return r.results[0]["out_x"].reshape(1, T, D)
```

```python
from contextlib import ExitStack

import concourse.bass as bass
from concourse import mybir

P = 128
T, D, F, E = 1024, 1024, 512, 16
HEADS, HD = 16, 64
TT, DC = T // P, D // P
GROUPS, EPG = 4, 4
CW = 31
EPS = 1e-6
PIECE = DC * 512
ADA = 12
FIRST_ADA = 4
REST_ADA = 2 * ADA - FIRST_ADA
MAXBLK = 32
TABLE = MAXBLK + 2
ADD_TAPS = 8


def trunk(nc, x, c_col, b_ada, final_g, vec_cols, b_out, b_router, w_router, w_ada, w_qkv, w_o, w_in, w_out,
          w_gate, w_up, w_down, out):
    f32, i32 = mybir.dt.float32, mybir.dt.int32
    ALU, ACT, AX = mybir.AluOpType, mybir.ActivationFunctionType, mybir.AxisListType
    ds = bass.ds

    mod_dram = nc.dram_tensor("mod_rows", (2 * 6 * D,), f32, kind="Internal").ap()
    h_dram = [nc.dram_tensor(f"h_rows{l}", (T, D), f32, kind="Internal").ap() for l in range(2)]
    y_dram = [nc.dram_tensor(f"expert_rows{l}", (MAXBLK * P, D), f32, kind="Internal").ap() for l in range(2)]

    ctx = ExitStack()
    with ctx:
        def sb(name, shape, dt=f32):
            return ctx.enter_context(nc.sbuf_tensor(name, shape, dt))

        def sem(name):
            return ctx.enter_context(nc.semaphore(name))

        xq = sb("xq", [P, TT, DC, P])
        kv = sb("kv", [P, 4 * PIECE])
        hT = sb("hT", [P, DC, T])
        ring = sb("ring", [P, 3, PIECE])
        bcA, bcB, bcC = sb("bcA", [P, D]), sb("bcB", [P, D]), sb("bcC", [P, D])
        pbuf = sb("pbuf", [P, 2, D + 2])
        oT = sb("oT", [P, DC, P])
        ident, ones, upper = sb("ident", [P, P]), sb("ones", [P, P]), sb("upper", [P, P])
        identb, maskb = sb("identb", [P, P], mybir.dt.bfloat16), sb("maskb", [P, P], mybir.dt.bfloat16)
        pace, eps = sb("pace", [P, 2]), sb("eps", [P, 1])
        half_ones = sb("half_ones", [P, 2, P])
        qstage = sb("qstage", [P, 2, P])
        cols = sb("cols", [P, 296 + 4 * DC])
        modc = sb("modc", [P, 4, 2, DC])
        cond = sb("cond", [P, DC])
        wr = sb("wr", [P, DC, E])
        brt = sb("brt", [P, E])
        ss, rstd = sb("ss", [P, TT]), sb("rstd", [P, TT])
        tokid = sb("tokid", [P, TT])
        pref_e, pref_g = sb("pref_e", [P, TT, E]), sb("pref_g", [P, TT, GROUPS])
        dest = sb("dest", [P, 2, TT], i32)
        wts = sb("wts", [P, 2, TT])
        bounds = sb("bounds", [1, E + 1], i32)
        slot_i = sb("slot_i", [P, 2, 2 * TT], i32)
        slot_tok = sb("slot_tok", [P, TABLE], i32)
        idx_now = sb("idx_now", [P, 1], i32)

        iota_i = qstage[:, 0, :].bitcast(i32)
        lane = half_ones[:, 0, :]
        ccol = cols[:, 0:8]
        b_in_c, w_dw_c = cols[:, 8:24], cols[:, 24:24 + 248].rearrange("p (c k) -> p c k", c=DC)
        b_dw_c, ln_g_c, ln_b_c = cols[:, 272:280], cols[:, 280:288], cols[:, 288:296]
        norm_c = cols[:, 296:296 + 4 * DC]
        hbuf = [pbuf[:, 0, 0:D], pbuf[:, 1, 0:D], bcA[:, :], bcB[:, :]]

        vslot = [kv[:, (2 + u) * PIECE:(3 + u) * PIECE] for u in range(2)]
        bias = oT[:, :, :].rearrange("p c t -> p (c t)").rearrange("p (u n) -> p u n", u=2)
        ada_sum = pbuf[:, :, 0:512]
        ada_out = bcA[:, :].rearrange("p (u n) -> p u n", u=2)
        kT = kv[:, 0:2 * PIECE].rearrange("p (c t) -> p c t", c=DC)
        vt = kv[:, 2 * PIECE:4 * PIECE].rearrange("p (s f) -> p s f", s=TT)
        beta, omega, prob, probT = hT[:, 0:2, :], hT[:, 2:4, :], hT[:, 4:6, :], hT[:, 6:8, :]
        cv = kT
        UW = T + CW - 1
        upad = kv[:, 2 * PIECE:2 * PIECE + 2 * UW].rearrange("p (b t) -> p b t", b=2)
        o_ = 2 * PIECE + 2 * UW
        usig = kv[:, o_:o_ + 2 * T].rearrange("p (b t) -> p b t", b=2)
        tapp = kv[:, o_ + 2 * T:o_ + 4 * T].rearrange("p (b t) -> p b t", b=2)
        acc2 = kv[:, o_ + 4 * T:o_ + 5 * T]
        hflat = hT[:, :, :].rearrange("p c t -> p (c t)")
        xg, xT = hflat[:, 0:1024], hflat[:, 1024:2048].rearrange("p (c t) -> p c t", c=DC)
        sg, ha, haT = hflat[:, 2048:2560], hflat[:, 2560:3072], hflat[:, 3072:3584]
        yo = hflat[:, 3584:4608]
        wset = [[ring[:, k, :] for k in range(3)], [kv[:, k * PIECE:(k + 1) * PIECE] for k in range(3)]]
        spare = kv[:, 3 * PIECE:4 * PIECE]
        ygat = [kv[:, 2 * D * b:2 * D * (b + 1)].rearrange("p (k d) -> p k d", k=2) for b in range(4)]
        low_hot = hflat[:, 4608:4608 + 2 * TT * P].rearrange("p (n q) -> p n q", q=P)
        high_hot = hflat[:, 6656:6656 + 2 * TT * TABLE].rearrange("p (n b) -> p n b", b=TABLE)

        def tmp(n, w=E):
            return spare[:, n * P:n * P + TT * w].rearrange("p (t e) -> p t e", t=TT)

        ps = ctx.enter_context(nc.psum_tensor("ps", [P, 8 * 512], f32))

        def bank(b, n=1):
            return ps[:, 512 * b:512 * (b + n)]

        const_made = sem("const_made")
        x_loaded, cols_loaded = sem("x_loaded"), sem("cols_loaded")
        cond_made = sem("cond_made")
        zeros_made = sem("zeros_made")
        ada_first = [sem(f"ada_first{n}") for n in range(FIRST_ADA)]
        ada_loaded = [sem(f"ada_loaded{u}") for u in range(2)]
        bias_loaded = [sem(f"bias_loaded{u}") for u in range(2)]
        row_stored = [sem(f"row_stored{u}") for u in range(2)]
        ada_used, ada_row, mod_stored = sem("ada_used"), sem("ada_row"), sem("mod_stored")
        bias_zeroed, ada_step, ada_summed, ada_reduced, row_kept = (
            sem("bias_zeroed"), sem("ada_step"), sem("ada_summed"), sem("ada_reduced"), sem("row_kept"))
        bc_loaded, gate_loaded, modc_loaded, modc_made = (sem("bc_loaded"), sem("gate_loaded"), sem("modc_loaded"),
                                                          sem("modc_made"))
        root_done = sem("root_done")
        sq_done, h_made, h_turned, h_kept, h_kept2 = (sem("sq_done"), sem("h_made"), sem("h_turned"), sem("h_kept"),
                                                      sem("h_kept2"))
        h_stored = [sem(f"h_stored{b}") for b in range(4)]
        at_loaded = [sem(f"at_loaded{j}") for j in range(8)]
        proj_done, proj_kept = sem("proj_done"), sem("proj_kept")
        q_staged, z_done, sig_done, omega_done, scanned = sem("q_staged"), sem("z_done"), sem("sig_done"), sem("omega_done"), sem("scanned")
        prob_made, prob_turned, probT_kept, av_done, o_kept = (sem("prob_made"), sem("prob_turned"),
                                                               sem("probT_kept"), sem("av_done"), sem("o_kept"))
        o_turned, oT_kept, wo_done, wo_scaled, x_again, x_made = (sem("o_turned"), sem("oT_kept"), sem("wo_done"),
                                                                  sem("wo_scaled"), sem("x_again"), sem("x_made"))
        edge_ready = sem("edge_ready")
        cv_loaded = [sem(f"cv_loaded{j}") for j in range(6)]
        in_done, usig_done, u_done, tap_made, tap_added, conv_done = (
            sem("in_done"), sem("usig_done"), sem("u_done"), sem("tap_made"), sem("tap_added"), sem("conv_done"))
        first_tap, dve_tap = sem("first_tap"), sem("dve_tap")
        mean_done, centered, squared, var_done, ln_root, ln_rstd, ln_scaled, ln_done = (
            sem("mean_done"), sem("centered"), sem("squared"), sem("var_done"), sem("ln_root"), sem("ln_rstd"),
            sem("ln_scaled"), sem("ln_done"))
        bout_loaded, out_done, out_used = sem("bout_loaded"), sem("out_done"), sem("out_used")
        both = lambda name: [sem(f"{name}{l}") for l in range(2)]
        logits_done, score_done, picked, counted, hot_made = (
            both("logits_done"), both("score_done"), both("picked"), both("counted"), both("hot_made"))
        bounds_made, table_summed, table_made = both("bounds_made"), both("table_summed"), both("table_made")
        w_loaded = [[[sem(f"w_loaded{l}{s}{k}") for k in range(3)] for s in range(2)] for l in range(2)]
        x_gathered, x_turned, xT_kept, xT_kept2 = (
            both("x_gathered"), both("x_turned"), both("xT_kept"), both("xT_kept2"))
        gate_done, up_done, silu_done, ha_made, ha_turned, haT_kept = (
            both("gate_done"), both("up_done"), both("silu_done"), both("ha_made"), both("ha_turned"), both("haT_kept"))
        down_done, y_kept = both("down_done"), both("y_kept")
        stored = both("stored")
        y_gathered = [[sem(f"y_gathered{l}{b}") for b in range(4)] for l in range(2)]
        x_added = both("x_added")
        dve_step = sem("dve_step")
        final_made, out_stored = sem("final_made"), [sem(f"out_stored{b}") for b in range(2)]

        block = ctx.enter_context(nc.Block())

        MOD = [(0, 0, 1, 2), (0, 3, 4, 5), (1, 0, 1, 2), (1, 3, 4, 5)]

        def reduced_after(cc):
            return 0 if cc < 1 else min(REST_ADA, (cc - 1) * REST_ADA // 13)

        def mod_row(l, j):
            return mod_dram[(6 * l + j) * D:(6 * l + j + 1) * D].partition_broadcast(P)

        def mod_col(l, j):
            return mod_dram[(6 * l + j) * D:(6 * l + j + 1) * D].rearrange("(c p) -> p c", p=P)

        def xtile(t):
            return xq[:, t, :, :].rearrange("p c j -> p (c j)")

        @block.sync
        def _(sp):
            sp.dma_start(xq[:, :, :, :].rearrange("p t c j -> p t (c j)"),
                         x.rearrange("(t p) d -> p t d", p=P)).then_inc(x_loaded, 16)
            for n in range(FIRST_ADA):
                if n >= 3:
                    sp.wait_ge(ada_used, n - 2)
                sp.dma_start(ring[:, (n + 2) % 3, :], w_ada[n]).then_inc(ada_first[n], 16)
            for j in range(8):
                if j < 3:
                    sp.wait_ge(ada_used, (2, 3, 4)[j])
                else:
                    sp.wait_ge(proj_done, (4, 8, 12, 16, 32)[j - 3])
                sp.dma_start(ring[:, j % 3, :], w_qkv[j] if j < 6 else w_o[j - 6]).then_inc(at_loaded[j], 16)
                if j == 2:
                    for u in range(2):
                        sp.dma_start(vslot[u], w_ada[FIRST_ADA + u]).then_inc(ada_loaded[u], 16)
                if 2 <= j <= 4:
                    with sp.Fori(*((1, 4), (4, 7), (7, REST_ADA // 2))[j - 2]) as i:
                        for u in range(2):
                            sp.wait_ge(ada_summed, 2 * i + u - 1)
                            sp.dma_start(vslot[u], w_ada[ds(2 * i + u + FIRST_ADA, 1)].rearrange("a p n -> (a p) n")
                                         ).then_inc(ada_loaded[u], 16)
            for l in range(2):
                sp.wait_ge(stored[l], 16)
            weights = (w_gate, w_up, w_down)

            def first_expert(l, s, k):
                sp.dma_start(wset[s][k], weights[k][l * E + s]).then_inc(w_loaded[l][s][k], 16)

            def experts(l):
                sp.wait_ge(bounds_made[l], 1)
                with sp.Fori(1, E // 2) as i:
                    for s in range(2):
                        ends = sp.value_load(bounds[0:1, ds(2 * i + s - 1, 1)], min_val=1, max_val=MAXBLK)
                        sp.wait_ge(down_done[l], 2 * ends)
                        for k, w in enumerate(weights):
                            sp.dma_start(wset[s][k], w[ds(2 * i + s + l * E, 1)].rearrange("a p n -> (a p) n")
                                         ).then_inc(w_loaded[l][s][k], 16)
                last = sp.value_load(bounds[0:1, E:E + 1], min_val=1, max_val=MAXBLK)
                sp.wait_ge(down_done[l], 2 * last)

            first_expert(0, 0, 2)
            sp.wait_ge(wo_done, TT)
            for k in range(2):
                first_expert(0, 0, k)
            sp.wait_ge(h_turned, 2 * TT)
            for k in range(3):
                first_expert(0, 1, k)
            experts(0)
            for j in range(6):
                if j >= 3:
                    sp.wait_ge(in_done, (4, 4, 8)[j - 3])
                sp.dma_start(ring[:, j % 3, :], w_in[j] if j < 4 else w_out[j - 4]).then_inc(cv_loaded[j], 16)
            first_expert(1, 0, 0)
            sp.wait_ge(ln_done, DC)
            for k in range(3):
                first_expert(1, 1, k)
            sp.wait_ge(out_done, 2 * TT)
            for k in range(1, 3):
                first_expert(1, 0, k)
            experts(1)
            for t in range(TT):
                sp.wait_ge(final_made, t + 1)
                sp.dma_start(out[t * P:(t + 1) * P, :], pbuf[:, t % 2, 0:D]).then_inc(out_stored[t % 2], 16)
            for b in range(2):
                sp.wait_ge(out_stored[b], 16 * TT // 2)

        @block.gpsimd
        def _(pool):
            kvrow = kv[0:1, 0:2 * D]
            pool.dma_start(cols[:, :], vec_cols).then_inc(cols_loaded, 16)
            pool.dma_start(kvrow, b_ada[:, 0:2 * D]).then_inc(cols_loaded, 16)
            pool.dma_start(wr[:, :, :], w_router).then_inc(cols_loaded, 16)
            pool.dma_start(brt[:, :], b_router.partition_broadcast(P)).then_inc(cols_loaded, 16)
            nc.gpsimd.memset(ident[:, :], 0.0)
            nc.gpsimd.memset(upper[:, :], 1.0)
            nc.gpsimd.memset(ones[:, :], 1.0)
            nc.gpsimd.memset(maskb[:, :], 0.0)
            nc.gpsimd.memset(eps[:, :], EPS)
            nc.gpsimd.memset(identb[:, :], 0.0)
            nc.gpsimd.memset(pbuf[:, :, D:D + 2], 1.0)
            nc.gpsimd.memset(half_ones[:, :, :], 1.0).then_inc(const_made, 1)
            pool.wait_ge(const_made, 1)
            nc.gpsimd.affine_select(out=ident[:, :], in_=ident[:, :], compare_op=ALU.not_equal, fill=1.0, base=0,
                                    pattern=[[-1, P]], channel_multiplier=1)
            nc.gpsimd.affine_select(out=half_ones[:, 0, :], in_=half_ones[:, 0, :], compare_op=ALU.is_gt, fill=0.0,
                                    base=HD, pattern=[[0, P]], channel_multiplier=-1)
            nc.gpsimd.affine_select(out=half_ones[:, 1, :], in_=half_ones[:, 1, :], compare_op=ALU.is_ge, fill=0.0,
                                    base=-HD, pattern=[[0, P]], channel_multiplier=1)
            nc.gpsimd.affine_select(out=maskb[:, :], in_=maskb[:, :], compare_op=ALU.is_gt, fill=-1e30, base=0,
                                    pattern=[[-1, P]], channel_multiplier=1)
            nc.gpsimd.affine_select(out=identb[:, :], in_=identb[:, :], compare_op=ALU.not_equal, fill=1.0, base=0,
                                    pattern=[[-1, P]], channel_multiplier=1)
            nc.gpsimd.affine_select(out=upper[:, :], in_=upper[:, :], compare_op=ALU.is_gt, fill=0.0, base=0,
                                    pattern=[[1, P]], channel_multiplier=-1).then_inc(const_made, 1)
            for n, (pattern, base, mul, width) in enumerate((([[P, TT]], 0, 1, TT), ([[0, TT], [-1, GROUPS]], GROUPS, 0,
                                                              TT * GROUPS), ([[0, TT], [-1, E]], E, 0, TT * E))):
                if n:
                    pool.wait_ge(dve_step, n)
                nc.gpsimd.iota(iota_i[:, 0:width], pattern=pattern, base=base, channel_multiplier=mul).then_inc(
                    const_made, 1)
            pool.wait_ge(ada_row, FIRST_ADA)
            pool.dma_start(mod_dram[0:2 * D].unsqueeze(0), kvrow).then_inc(mod_stored, 16)
            pool.wait_ge(mod_stored, 16)

            def load_modc(n):
                l, shift, scale, gate = MOD[n]
                with nc.allow_non_contiguous_dma("a vector by its chunks, to columns"):
                    pool.dma_start(modc[:, n, 0, :], mod_col(l, shift)).then_inc(modc_loaded, 16)
                    pool.dma_start(modc[:, n, 1, :], mod_col(l, scale)).then_inc(modc_loaded, 16)

            def load_gate(l, j):
                pool.dma_start(bcC[:, :], mod_row(l, j)).then_inc(gate_loaded, 16)

            def store_h(n, t):
                pool.wait_ge(h_made, TT * n + t + 1)
                pool.dma_start(h_dram[n // 2][t * P:(t + 1) * P, :], hbuf[t % 4]).then_inc(h_stored[t % 4], 16)

            load_modc(0)
            pool.wait_ge(bias_zeroed, 1)
            for n in range(REST_ADA + 2):
                u = n % 2
                if n < REST_ADA:
                    if n >= 2:
                        pool.wait_ge(ada_summed, n - 1)
                    pool.dma_start(bias[0:1, u, :], b_ada[:, 512 * (FIRST_ADA + n):512 * (FIRST_ADA + n + 1)]
                                   ).then_inc(bias_loaded[u], 16)
                if n >= 2:
                    m = FIRST_ADA + n - 2
                    pool.wait_ge(row_kept, n - 1)
                    pool.dma_start(mod_dram[512 * m:512 * (m + 1)].unsqueeze(0), ada_out[0:1, u, :]
                                   ).then_inc(row_stored[u], 16)
            for u in range(2):
                pool.wait_ge(row_stored[u], 16 * REST_ADA // 2)
            for n in range(1, 4):
                load_modc(n)
            load_gate(0, 2)

            def stage(qb, chunk, u):
                nc.gpsimd.tensor_tensor(qstage[:, u, :], xq[:, qb, ds(chunk, 1), :].rearrange("p a t -> p (a t)"),
                                        half_ones[:, u, :], ALU.mult).then_inc(q_staged, 1)

            pool.wait_ge(proj_kept, 16)
            stage(0, 0, 0)
            stage(0, 0, 1)
            for qb in range(TT):
                with pool.Fori(0, HEADS // 2 - 1) as i:
                    for u in range(2):
                        g = 16 * qb + 2 * i + u
                        pool.wait_ge(z_done, g + 1)
                        nc.gpsimd.tensor_tensor(pace[:, u:u + 1], ones[:, 0:1], ones[:, 0:1], ALU.mult)
                        stage(qb, i + 1, u)
                if qb:
                    pool.wait_ge(x_made, qb)
                pool.dma_start(bcB[:, :], x[qb * P:(qb + 1) * P, :]).then_inc(x_again, 16)
                if qb in (3, 4):
                    if qb == 3:
                        pool.wait_ge(zeros_made, 1)
                    pool.dma_start(y_dram[qb - 3][E * P:, :].rearrange("(b p) d -> p b d", p=P),
                                   ring[:, 2, 0:D].unsqueeze(1).to_broadcast([P, MAXBLK - E, D])).then_inc(
                                       stored[qb - 3], 16)
                for u in range(2):
                    if qb < TT - 1:
                        pool.wait_ge(z_done, 16 * qb + 14 + u + 1)
                        stage(qb + 1, 0, u)

            def moe(l):
                pool.wait_ge(table_made[l], 1)
                for b in range(4):
                    pool.wait_ge(h_stored[b], 16 * TT // 4 * (l + 1))
                if l:
                    pool.dma_start(bcA[:, :], final_g.partition_broadcast(P)).then_inc(bc_loaded, 16)

                def gather(b):
                    nc.gpsimd.tensor_copy(idx_now[:, :], slot_tok[:, ds(b, 1)])
                    pool.drain()
                    pool.indirect_dma_start(
                        out=xg, out_offset=None, in_=h_dram[l],
                        in_offset=bass.IndirectOffsetOnAxis(ap=idx_now[:, 0:1], axis=0)).then_inc(x_gathered[l], 16)

                gather(0)
                pool.wait_ge(x_turned[l], 1)
                gather(1)
                blocks = pool.value_load(bounds[0:1, E:E + 1], min_val=1, max_val=MAXBLK)
                with pool.Fori(0, blocks) as b:
                    pool.wait_ge(x_turned[l], b + 2)
                    gather(b + 2)
                    pool.wait_ge(y_kept[l], 2 * b + 2)
                    pool.dma_start(y_dram[l][ds(b * P, P), :], yo).then_inc(stored[l], 16)
                    pool.wait_ge(x_gathered[l], 16 * b + 48)
                    pool.wait_ge(stored[l], 16 * b + 32)
                for t in range(TT):
                    if t >= 4:
                        pool.wait_ge(x_added[l], t - 3)
                    for k in range(2):
                        pool.indirect_dma_start(
                            out=ygat[t % 4][:, k, :], out_offset=None, in_=y_dram[l],
                            in_offset=bass.IndirectOffsetOnAxis(ap=dest[:, k, t:t + 1], axis=0)
                        ).then_inc(y_gathered[l][t % 4], 16)

            pool.wait_ge(x_made, TT)
            nc.gpsimd.iota(iota_i, pattern=[[1, P]], base=0, channel_multiplier=0).then_inc(const_made, 1)
            for t in range(TT):
                store_h(1, t)
            load_gate(0, 5)
            moe(0)
            load_gate(1, 2)
            for c in range(DC):
                for j in range(1, ADD_TAPS):
                    pool.wait_ge(tap_made, c * ADD_TAPS + j + 1)
                    nc.gpsimd.tensor_tensor(acc2, acc2, tapp[:, j % 2, :], ALU.add).then_inc(tap_added, 1)
                    if j < ADD_TAPS - 1:
                        pool.wait_ge(tap_added, c * (ADD_TAPS - 1) + j)
            pool.wait_ge(ln_done, DC)
            pool.dma_start(tapp[:, 0, :], b_out.partition_broadcast(P)).then_inc(bout_loaded, 16)
            for t in range(TT):
                store_h(3, t)
            pool.wait_ge(out_used, 2 * TT)
            load_gate(1, 5)
            moe(1)

        @block.scalar
        def _(act):
            act.wait_ge(cols_loaded, 64)
            nc.scalar.activation(cond[:, :], ccol, ACT.Silu).then_inc(cond_made, 1)

            def square(n, t):
                nc.scalar.activation(oT[:, :, :].rearrange("p c t -> p (c t)"), xtile(t), ACT.Square,
                                     accum_out=ss[:, t:t + 1]).then_inc(sq_done, 1)
                act.wait_ge(sq_done, TT * n + t + 1)

            def roots(n, t, tiles=1):
                nc.scalar.activation(rstd[:, t:t + tiles], ss[:, t:t + tiles], ACT.Sqrt, bias=eps[:, :],
                                     scale=1.0 / D).then_inc(root_done, tiles)

            def norm_keep(n, t):
                act.wait_ge(h_turned, TT * n + t + 1)
                for c in range(4):
                    ins = nc.scalar.activation(hT[:, c, t * P:(t + 1) * P], bank(2 * (t % 2))[:, c * P:(c + 1) * P],
                                               ACT.Identity, bias=modc[:, n, 0, c:c + 1],
                                               scale=modc[:, n, 1, c:c + 1])
                ins.then_inc(h_kept, 1)

            def keep_row(n):
                if n >= 2:
                    act.wait_ge(row_stored[n % 2], 16 * (n // 2))
                act.wait_ge(ada_reduced, n + 1)
                nc.scalar.activation(ada_out[0:1, n % 2, :], bank(4 + n % 2)[0:1, :], ACT.Copy).then_inc(row_kept, 1)

            act.wait_ge(const_made, 2)
            act.wait_ge(x_loaded, 16)
            for t in range(TT):
                square(0, t)
            roots(0, 0, TT)
            act.wait_ge(modc_made, 1)
            for t in range(TT):
                norm_keep(0, t)
            kept = 0
            for cc in range(16):
                while kept < reduced_after(cc - 1):
                    keep_row(kept)
                    kept += 1
                act.wait_ge(proj_done, cc + 1)
                src = bank(2 * (cc % 2), 2)
                if cc < 8:
                    nc.scalar.activation(xq[:, :, cc, :], src.rearrange("p (t j) -> p t j", t=TT),
                                         ACT.Copy).then_inc(proj_kept, 1)
                else:
                    nc.scalar.activation(kT[:, cc - 8, :], src, ACT.Copy).then_inc(proj_kept, 1)
            while kept < REST_ADA:
                keep_row(kept)
                kept += 1
            act.wait_ge(ada_summed, REST_ADA)
            for t in range(TT):
                act.wait_ge(proj_done, 16 + 2 * (t + 1))
                nc.scalar.activation(vt[:, t, :], bank(2 * (t % 2), 2), ACT.Copy).then_inc(proj_kept, 1)

            def sigmoids(qb, g, u, early=False):
                w = (qb + 1) * P
                act.wait_ge(z_done, g + 1)
                if not early:
                    act.wait_ge(scanned, g - 1)
                nc.scalar.activation(omega[:, u, 0:w], bank(2 * u, 2)[:, 0:w], ACT.Sigmoid,
                                     scale=-HD ** -0.5).then_inc(omega_done, 1)
                if not early:
                    act.wait_ge(prob_made, g - 1)
                nc.scalar.activation(beta[:, u, 0:w], bank(2 * u, 2)[:, 0:w], ACT.Sigmoid,
                                     scale=HD ** -0.5).then_inc(sig_done, 1)

            def keep_turned(qb, g, u):
                w = (qb + 1) * P
                act.wait_ge(prob_turned, g + 1)
                nc.scalar.activation(probT[:, u, 0:w], bank(4, 2)[:, 0:w], ACT.Copy).then_inc(probT_kept, 1)

            sigmoids(0, 0, 0, early=True)
            sigmoids(0, 1, 1, early=True)
            for qb in range(TT):
                with act.Fori(0, HEADS // 2 - 1) as i:
                    for u in range(2):
                        g = 16 * qb + 2 * i + u
                        sigmoids(qb, g + 2, u)
                        keep_turned(qb, g, u)
                for u in range(2):
                    g = 16 * qb + 14 + u
                    if qb < TT - 1:
                        sigmoids(qb + 1, g + 2, u)
                    keep_turned(qb, g, u)
                if qb:
                    act.wait_ge(x_made, qb)
                    square(1, qb - 1)
                for half in range(2):
                    act.wait_ge(o_turned, 2 * qb + half + 1)
                    nc.scalar.activation(oT[:, 4 * half:4 * half + 4, :],
                                         bank(7).rearrange("p (c t) -> p c t", c=4), ACT.Copy).then_inc(oT_kept, 1)

            def moe(l):
                act.wait_ge(logits_done[l], TT)
                nc.scalar.activation(tmp(0), bank(4)[:, 0:TT * E].rearrange("p (t e) -> p t e", t=TT),
                                     ACT.Sigmoid).then_inc(score_done[l], 1)

                def keep(b):
                    act.wait_ge(x_turned[l], b + 1)
                    for c in range(4):
                        ins = nc.scalar.activation(xT[:, c, :], bank(2)[:, c * P:(c + 1) * P], ACT.Identity,
                                                   bias=modc[:, 2 * l + 1, 0, c:c + 1],
                                                   scale=modc[:, 2 * l + 1, 1, c:c + 1])
                    ins.then_inc(xT_kept[l], 1)

                keep(0)
                blocks = act.value_load(bounds[0:1, E:E + 1], min_val=1, max_val=MAXBLK)
                with act.Fori(0, blocks) as b:
                    act.wait_ge(gate_done[l], b + 1)
                    nc.scalar.activation(sg, bank(0), ACT.Silu).then_inc(silu_done[l], 1)
                    act.wait_ge(up_done[l], 2 * b + 2)
                    keep(b + 1)

            act.wait_ge(x_made, TT)
            square(1, TT - 1)
            roots(1, 0, TT)
            act.wait_ge(modc_made, 4)
            for t in range(TT):
                norm_keep(1, t)
            moe(0)
            for t in range(TT + 2):
                if t < TT:
                    act.wait_ge(x_added[0], t + 1)
                    square(2, t)
                    roots(2, t)
                if t >= 2:
                    norm_keep(2, t - 2)
            for c in range(DC):
                g = 4 * (c % 2)
                act.wait_ge(in_done, c + 1)
                nc.scalar.activation(usig[:, c % 2, :], bank(g + 2, 2), ACT.Sigmoid,
                                     bias=b_in_c[:, 8 + c:9 + c]).then_inc(usig_done, 1)
                act.wait_ge(u_done, c + 1)
                for j in range(ADD_TAPS):
                    if j == 0:
                        if c:
                            act.wait_ge(conv_done, c)
                        dst = acc2
                    else:
                        if c or j > 2:
                            act.wait_ge(tap_added, c * (ADD_TAPS - 1) + max(j - 2, 0))
                        dst = tapp[:, j % 2, :]
                    nc.scalar.activation(dst, upad[:, c % 2, j:j + T], ACT.Copy,
                                         scale=w_dw_c[:, c, j:j + 1]).then_inc(tap_made, 1)
            for c in range(DC):
                act.wait_ge(centered, c + 1)
                if c >= 2:
                    act.wait_ge(var_done, c - 1)
                nc.scalar.activation(usig[:, c % 2, :], cv[:, c, :], ACT.Square).then_inc(squared, 1)
            act.wait_ge(ln_root, 1)
            nc.scalar.activation(tapp[:, 0, :], tapp[:, 1, :], ACT.Sqrt).then_inc(ln_root, 1)
            for c in range(DC):
                act.wait_ge(ln_scaled, c + 1)
                nc.scalar.activation(hT[:, c, :], cv[:, c, :], ACT.Silu, bias=ln_b_c[:, c:c + 1],
                                     scale=ln_g_c[:, c:c + 1]).then_inc(ln_done, 1)
            for t in range(TT + 1):
                if t < TT:
                    act.wait_ge(out_used, 2 * t + 2)
                    square(3, t)
                    roots(3, t)
                if t >= 1:
                    norm_keep(3, t - 1)
            moe(1)
            for t in range(TT):
                act.wait_ge(x_added[1], t + 1)
                square(4, t)
                roots(4, t)

        @block.vector
        def _(dve):
            steps = [0]

            def step(ins):
                steps[0] += 1
                ins.then_inc(dve_step, 1)
                dve.wait_ge(dve_step, steps[0])

            V = nc.vector
            for n, dst in enumerate((tokid[:, :], pref_g[:, :, :].rearrange("p t g -> p (t g)"),
                                     pref_e[:, :, :].rearrange("p t e -> p (t e)"))):
                dve.wait_ge(const_made, 3 + n)
                step(V.tensor_copy(dst, iota_i[:, 0:dst.shape[1]]))

            def norm_scale(n, t):
                dve.wait_ge(root_done, TT * n + t + 1)
                step(V.reciprocal(rstd[:, t:t + 1], rstd[:, t:t + 1]))
                if n == 4:
                    if t >= 2:
                        dve.wait_ge(out_stored[t % 2], 16 * (t // 2))
                    V.scalar_tensor_tensor(hbuf[t % 2], xtile(t), rstd[:, t:t + 1], bcA[:, :], ALU.mult,
                                           ALU.mult).then_inc(final_made, 1)
                    return
                if t >= 4:
                    dve.wait_ge(h_turned, TT * n + t - 3)
                    if n % 2:
                        dve.wait_ge(h_stored[t % 4], 16 * (TT // 4 * (n // 2) + t // 4))
                V.tensor_scalar(hbuf[t % 4], xtile(t), rstd[:, t:t + 1], None, ALU.mult).then_inc(h_made, 1)

            def norm_keep(n, t):
                dve.wait_ge(h_turned, TT * n + t + 1)
                for c in range(4, DC):
                    ins = V.tensor_scalar(hT[:, c, t * P:(t + 1) * P], bank(2 * (t % 2) + 1)[:, (c - 4) * P:(c - 3) * P],
                                          modc[:, n, 1, c:c + 1], modc[:, n, 0, c:c + 1], ALU.mult, ALU.add)
                ins.then_inc(h_kept2, 1)

            def make_modc(n):
                V.scalar_tensor_tensor(modc[:, n, 1, :], modc[:, n, 1, :], 1.0, norm_c[:, DC * n:DC * (n + 1)],
                                       ALU.add, ALU.mult).then_inc(modc_made, 1)

            for t in range(4):
                norm_scale(0, t)
            dve.wait_ge(cols_loaded, 64)
            for n in range(FIRST_ADA):
                dve.wait_ge(ada_used, n + 1)
                at = kv[0:1, 512 * n:512 * n + 512]
                V.tensor_tensor(at, bank(n)[0:1, :], at, ALU.add).then_inc(ada_row, 1)
            dve.wait_ge(modc_loaded, 32)
            make_modc(0)
            dve.wait_ge(modc_made, 1)
            for t in range(TT):
                if t >= 4:
                    norm_scale(0, t)
                norm_keep(0, t)
            V.memset(oT[:, :, :], 0.0).then_inc(bias_zeroed, 1)
            dve.wait_ge(h_turned, TT)

            def sum_pieces(i, first=False):
                for u in range(2):
                    dve.wait_ge(ada_loaded[u], 16 * i + 16)
                    dve.wait_ge(bias_loaded[u], 16 * i + 16)
                    if not first:
                        dve.wait_ge(ada_reduced, 2 * i + u - 1)
                    for c in range(DC):
                        if c:
                            dve.wait_ge(ada_step, 14 * i + 7 * u + c)
                        ins = V.scalar_tensor_tensor(ada_sum[:, u, :], vslot[u][:, 512 * c:512 * c + 512],
                                                     cond[:, c:c + 1], ada_sum[:, u, :] if c else bias[:, u, :],
                                                     ALU.mult, ALU.add)
                        ins.then_inc(ada_step if c < DC - 1 else ada_summed, 1)

            sum_pieces(0, first=True)
            with dve.Fori(1, REST_ADA // 2) as i:
                sum_pieces(i)

            def probabilities(qb, g, u, early=False):
                w = (qb + 1) * P
                dve.wait_ge(omega_done, g + 1)
                V.tensor_tensor_scan(pbuf[:, u, D - w:D][:, ::-1], omega[:, u, 0:w][:, ::-1], omega[:, u, 0:w], 1.0,
                                     ALU.mult, ALU.bypass).then_inc(scanned, 1)
                dve.wait_ge(scanned, g + 1)
                dve.wait_ge(sig_done, g + 1)
                if not early:
                    dve.wait_ge(prob_turned, g - 1)
                V.tensor_tensor(prob[:, u, 0:w], beta[:, u, 0:w], pbuf[:, u, D - w + 1:D + 1],
                                ALU.mult).then_inc(prob_made, 1)

            def keep_o(pair, chunk):
                dve.wait_ge(av_done, 2 * pair + 2)
                V.tensor_copy(bcA[:, ds(chunk * P, P)], bank(6)[:, 0:P]).then_inc(o_kept, 1)

            def add_projection(qb):
                dve.wait_ge(wo_done, qb + 1)
                dve.wait_ge(gate_loaded, 16)
                dve.wait_ge(x_again, 16 * (qb + 1))
                V.tensor_tensor(bcA[:, :], bank(4, 2), bcC[:, :], ALU.mult).then_inc(wo_scaled, 1)
                dve.wait_ge(wo_scaled, qb + 1)
                V.tensor_tensor(xq[:, qb, :, :].rearrange("p c j -> p (c j)"), bcA[:, :], bcB[:, :],
                                ALU.add).then_inc(x_made, 1)

            dve.wait_ge(proj_done, 32)
            V.memset(ring[:, 2, 0:D], 0.0).then_inc(zeros_made, 1)
            for qb in range(TT):
                if qb == 1:
                    dve.wait_ge(modc_loaded, 128)
                    for n in range(1, 4):
                        make_modc(n)
                for u in range(2):
                    probabilities(qb, 16 * qb + u, u, early=(qb == 0))
                if qb:
                    add_projection(qb - 1)
                with dve.Fori(1, HEADS // 2) as i:
                    for u in range(2):
                        probabilities(qb, 16 * qb + 2 * i + u, u)
                    keep_o(8 * qb + i - 1, i - 1)
                keep_o(8 * qb + 7, 7)
            add_projection(TT - 1)

            def moe(l):
                sc, sel, a, b, m0, m1, both_ = (tmp(n) for n in (0, 1, 2, 3, 4, 5, 6))
                gs, g1, g2, g3 = (tmp(n, GROUPS) for n in (7, 8, 9, 10))
                one = lambda n: tmp(n, 1)

                def wide(ap, w):
                    return ap.to_broadcast([P, TT, w])

                dve.wait_ge(score_done[l], 1)
                dve.wait_ge(cols_loaded, 64)
                step(V.tensor_tensor(sel, sc, brt[:, :].unsqueeze(1).to_broadcast([P, TT, E]), ALU.add))
                s4 = sel.rearrange("p t (g e) -> p t g e", e=EPG)
                r = [s4[:, :, :, j] for j in range(EPG)]
                V.tensor_tensor(gs, r[0], r[1], ALU.max)
                V.tensor_tensor(g1, r[0], r[1], ALU.min)
                V.tensor_tensor(g2, r[2], r[3], ALU.max)
                step(V.tensor_tensor(g3, r[2], r[3], ALU.min))
                step(V.tensor_tensor(g1, g1, g3, ALU.max))
                step(V.tensor_tensor(g3, gs, g2, ALU.min))
                step(V.tensor_tensor(gs, gs, g2, ALU.max))
                step(V.tensor_tensor(g1, g1, g3, ALU.max))
                step(V.tensor_tensor(gs, gs, g1, ALU.add))

                def first_largest(dst, src, prefer, w, scratch, top):
                    step(V.tensor_reduce(top, src, AX.X, ALU.max))
                    step(V.tensor_tensor(scratch, src, wide(top, w), ALU.is_equal))
                    step(V.tensor_tensor(scratch, scratch, prefer, ALU.mult))
                    step(V.tensor_reduce(top, scratch, AX.X, ALU.max))
                    step(V.tensor_tensor(dst, scratch, wide(top, w), ALU.is_equal))

                first_largest(g2, gs, pref_g[:, :, :], GROUPS, g1, one(11))
                step(V.tensor_scalar(g3, g2, -1.0, 1e30, ALU.add, ALU.mult))
                a4, w4 = a.rearrange("p t (g e) -> p t g e", e=EPG), [P, TT, GROUPS, EPG]
                for j in range(EPG):
                    V.tensor_tensor(a4[:, :, :, j], r[j], g2, ALU.mult)
                step(V.memset(both_, 0.0))
                for j in range(EPG):
                    ins = V.tensor_tensor(a4[:, :, :, j], a4[:, :, :, j], g3, ALU.add)
                step(ins)
                first_largest(m0, a, pref_e[:, :, :], E, b, one(11))
                step(V.tensor_scalar(b, m0, -1e30, None, ALU.mult))
                step(V.tensor_tensor(a, a, b, ALU.add))
                first_largest(m1, a, pref_e[:, :, :], E, b, one(11))
                step(V.tensor_tensor(both_, m0, m1, ALU.add))
                run = spare[:, 12 * P:12 * P + (TT + 1) * E].rearrange("p (t e) -> p t e", e=E)
                step(V.memset(run[:, 0, :], 0.0))
                for t in range(TT):
                    step(V.tensor_tensor(run[:, t + 1, :], run[:, t, :], both_[:, t, :], ALU.add))
                V.tensor_copy(b, both_).then_inc(picked[l], 1)
                dve.wait_ge(counted[l], 1)
                dest_f, slot_f = dest[:, :, :].rearrange("p k t -> p (k t)"), spare[:, 18 * P:18 * P + 4 * TT].rearrange(
                    "p (h n) -> p h n", h=2)
                cnt, nb, cum, zero = (spare[:, (14 + n) * P:(14 + n) * P + E] for n in range(4))
                step(V.memset(nb, 1.0))
                step(V.memset(zero, 0.0))
                step(V.tensor_copy(cnt, bank(5)[:, P:P + E]))
                for j in range(1, T // P):
                    step(V.scalar_tensor_tensor(nb, cnt, float(j * P), nb, ALU.is_gt, ALU.add))
                step(V.tensor_tensor_scan(cum, nb, zero, 0.0, ALU.add, ALU.add))
                V.memset(bounds[:, :], 0)
                V.tensor_tensor(nb, cum, nb, ALU.subtract).then_inc(dve_step, 1)
                steps[0] += 1
                dve.wait_ge(dve_step, steps[0])
                V.tensor_copy(bounds[:, 1:E + 1], cum[0:1, :]).then_inc(bounds_made[l], 1)
                step(V.tensor_scalar(nb, nb, float(P), None, ALU.mult))
                step(V.tensor_tensor(b, bank(5)[:, 0:P].rearrange("p (t e) -> p t e", t=TT),
                                     nb.unsqueeze(1).to_broadcast([P, TT, E]), ALU.add))
                for k, m in enumerate((m0, m1)):
                    step(V.tensor_tensor(a, b, m, ALU.mult))
                    step(V.tensor_reduce(one(11)[:, :, 0], a, AX.X, ALU.add))
                    step(V.tensor_copy(dest[:, k, :], one(11)[:, :, 0]))
                step(V.tensor_single_scalar(slot_i[:, 0, :], dest_f, P - 1, ALU.bitwise_and))
                step(V.tensor_single_scalar(slot_i[:, 1, :], dest_f, P.bit_length() - 1, ALU.arith_shift_right))
                step(V.tensor_copy(slot_f, slot_i[:, :, :]))
                V.tensor_tensor(low_hot, lane.unsqueeze(1).to_broadcast([P, 2 * TT, P]),
                                slot_f[:, 0, :].unsqueeze(2).to_broadcast([P, 2 * TT, P]), ALU.is_equal)
                step(V.tensor_tensor(high_hot, lane[:, 0:TABLE].unsqueeze(1).to_broadcast([P, 2 * TT, TABLE]),
                                     slot_f[:, 1, :].unsqueeze(2).to_broadcast([P, 2 * TT, TABLE]), ALU.is_equal))
                for k in range(2):
                    part = high_hot[:, TT * k:TT * (k + 1), :]
                    V.tensor_tensor(part, part, tokid[:, :].unsqueeze(2).to_broadcast([P, TT, TABLE]),
                                    ALU.mult).then_inc(hot_made[l], 1)
                dve.wait_ge(table_summed[l], 1)
                V.tensor_copy(slot_tok[:, :], bank(6)[:, 0:TABLE]).then_inc(table_made[l], 1)
                for k, m in enumerate((m0, m1)):
                    step(V.tensor_tensor(a, sc, m, ALU.mult))
                    step(V.tensor_reduce(wts[:, k, :], a, AX.X, ALU.add))
                step(V.tensor_tensor(one(11)[:, :, 0], wts[:, 0, :], wts[:, 1, :], ALU.add))
                step(V.reciprocal(one(11)[:, :, 0], one(11)[:, :, 0]))
                for k in range(2):
                    step(V.tensor_tensor(wts[:, k, :], wts[:, k, :], one(11)[:, :, 0], ALU.mult))

                def keep(b):
                    dve.wait_ge(x_turned[l], b + 1)
                    for c in range(4, DC):
                        ins = V.tensor_scalar(xT[:, c, :], bank(3)[:, (c - 4) * P:(c - 3) * P],
                                              modc[:, 2 * l + 1, 1, c:c + 1], modc[:, 2 * l + 1, 0, c:c + 1],
                                              ALU.mult, ALU.add)
                    ins.then_inc(xT_kept2[l], 1)

                keep(0)
                dve.wait_ge(gate_loaded, 16 * (2 * l + 2))
                blocks = dve.value_load(bounds[0:1, E:E + 1], min_val=1, max_val=MAXBLK)
                with dve.Fori(0, blocks) as n:
                    dve.wait_ge(silu_done[l], n + 1)
                    for f in range(2):
                        dve.wait_ge(up_done[l], 2 * n + f + 1)
                        at = slice(256 * f, 256 * f + 256)
                        V.tensor_tensor(ha[:, at], sg[:, at], bank((1, 7)[f])[:, 0:256], ALU.mult).then_inc(
                            ha_made[l], 1)
                    for f in range(2):
                        dve.wait_ge(ha_turned[l], 2 * n + f + 1)
                        V.tensor_copy(haT[:, 256 * f:256 * f + 256], bank((4, 0)[f])[:, 0:256]).then_inc(haT_kept[l], 1)
                    keep(n + 1)
                    dve.wait_ge(stored[l], 16 * n + 16)
                    for f in range(2):
                        dve.wait_ge(down_done[l], 2 * n + f + 1)
                        V.tensor_tensor(yo[:, 512 * f:512 * f + 512], bank(5 + f), bcC[:, 512 * f:512 * f + 512],
                                        ALU.mult).then_inc(y_kept[l], 1)

            def combine(l, t):
                dve.wait_ge(y_gathered[l][t % 4], 32 * (t // 4 + 1))
                step(V.scalar_tensor_tensor(xtile(t), ygat[t % 4][:, 0, :], wts[:, 0, t:t + 1], xtile(t), ALU.mult,
                                            ALU.add))
                V.scalar_tensor_tensor(xtile(t), ygat[t % 4][:, 1, :], wts[:, 1, t:t + 1], xtile(t), ALU.mult,
                                       ALU.add).then_inc(x_added[l], 1)

            dve.wait_ge(const_made, 6)
            V.tensor_copy(lane, iota_i)
            for t in range(TT):
                norm_scale(1, t)
                if t:
                    norm_keep(1, t - 1)
            norm_keep(1, TT - 1)
            moe(0)
            for t in range(TT + 2):
                if t < TT:
                    combine(0, t)
                if 1 <= t <= TT:
                    norm_scale(2, t - 1)
                if t >= 2:
                    norm_keep(2, t - 2)
            step(V.memset(upad[:, :, 0:CW - 1], 0.0))
            for c in range(DC):
                g = 4 * (c % 2)
                dve.wait_ge(usig_done, c + 1)
                u = upad[:, c % 2, :]
                V.scalar_tensor_tensor(u[:, CW - 1:UW], bank(g, 2), b_in_c[:, c:c + 1], usig[:, c % 2, :], ALU.add,
                                       ALU.mult).then_inc(u_done, 1)
                dve.wait_ge(u_done, c + 1)
                step(V.tensor_scalar(cv[:, c, :], u[:, ADD_TAPS:ADD_TAPS + T], w_dw_c[:, c, ADD_TAPS:ADD_TAPS + 1],
                                     b_dw_c[:, c:c + 1], ALU.mult, ALU.add))
                for k in range(ADD_TAPS + 1, CW):
                    step(V.scalar_tensor_tensor(cv[:, c, :], u[:, k:k + T], w_dw_c[:, c, k:k + 1], cv[:, c, :],
                                                ALU.mult, ALU.add))
                dve.wait_ge(tap_added, (c + 1) * (ADD_TAPS - 1))
                V.tensor_tensor(cv[:, c, :], cv[:, c, :], acc2, ALU.add).then_inc(conv_done, 1)
            dve.wait_ge(mean_done, 1)
            step(V.tensor_scalar(usig[:, 0, :], bank(0, 2), 1.0 / D, None, ALU.mult))
            step(V.tensor_copy(acc2, usig[:, 0, :]))
            for c in range(DC):
                V.tensor_tensor(cv[:, c, :], cv[:, c, :], acc2, ALU.subtract).then_inc(centered, 1)
            dve.wait_ge(var_done, DC)
            V.tensor_scalar(tapp[:, 1, :], bank(2, 2), 1.0 / D, EPS, ALU.mult, ALU.add).then_inc(ln_root, 1)
            dve.wait_ge(ln_root, 2)
            step(V.reciprocal(tapp[:, 0, :], tapp[:, 0, :]))
            for c in range(DC):
                V.tensor_tensor(cv[:, c, :], cv[:, c, :], tapp[:, 0, :], ALU.mult).then_inc(ln_scaled, 1)
            dve.wait_ge(bout_loaded, 16)
            dve.wait_ge(gate_loaded, 16 * 3)
            for t in range(TT):
                for half in range(2):
                    n = 2 * t + half
                    cs = slice(512 * half, 512 * half + 512)
                    dve.wait_ge(out_done, n + 1)
                    y = acc2[:, cs]
                    step(V.tensor_tensor(y, bank(5 + n % 3), tapp[:, 0, cs], ALU.add))
                    step(V.tensor_tensor(y, y, bcC[:, cs], ALU.mult))
                    xt = xq[:, t, 4 * half:4 * half + 4, :].rearrange("p c j -> p (c j)")
                    V.tensor_tensor(xt, xt, y, ALU.add).then_inc(out_used, 1)
                norm_scale(3, t)
                if t:
                    norm_keep(3, t - 1)
            norm_keep(3, TT - 1)
            moe(1)
            dve.wait_ge(bc_loaded, 16)
            for t in range(TT + 1):
                if t < TT:
                    combine(1, t)
                if t:
                    norm_scale(4, t - 1)

        @block.tensor
        def _(pe):
            mm = nc.tensor.matmul
            pe.wait_ge(cond_made, 1)
            for n in range(FIRST_ADA):
                pe.wait_ge(ada_first[n], 16)
                for c in range(DC):
                    ins = mm(bank(n)[0:1, :], cond[:, c:c + 1], ring[:, (n + 2) % 3, 512 * c:512 * c + 512],
                             start=(c == 0), stop=(c == DC - 1))
                ins.then_inc(ada_used, 1)
            pe.wait_ge(ada_row, FIRST_ADA)
            pe.wait_ge(const_made, 2)

            def turn(n, t):
                pe.wait_ge(h_made, TT * n + t + 1)
                if t >= 2:
                    pe.wait_ge(h_kept, TT * n + t - 1)
                    pe.wait_ge(h_kept2, TT * n + t - 1)
                for c in range(DC):
                    ins = nc.tensor.transpose(bank(2 * (t % 2), 2)[:, c * P:(c + 1) * P],
                                              hbuf[t % 4][:, c * P:(c + 1) * P], ident[:, :])
                ins.then_inc(h_turned, 1)

            def turned(n, t):
                pe.wait_ge(h_kept, TT * n + t + 1)
                pe.wait_ge(h_kept2, TT * n + t + 1)

            def logits(n, t):
                turned(n, t)
                for c in range(DC):
                    ins = mm(bank(4)[:, E * t:E * t + E], hT[:, c, t * P:(t + 1) * P], wr[:, c, :],
                             start=(c == 0), stop=(c == DC - 1))
                ins.then_inc(logits_done[n // 2], 1)

            for t in range(TT):
                turn(0, t)
            turned(0, TT - 1)
            reduced = 0
            for cc in range(16):
                j, q = cc // 4, cc % 4
                if q == 0:
                    pe.wait_ge(at_loaded[j], 16)
                if cc >= 2:
                    pe.wait_ge(proj_kept, cc - 1)
                for half in range(2):
                    for c in range(DC):
                        ins = mm(bank(2 * (cc % 2) + half), ring[:, j % 3, 512 * c + P * q:512 * c + P * q + P],
                                 hT[:, c, 512 * half:512 * half + 512], start=(c == 0), stop=(c == DC - 1))
                ins.then_inc(proj_done, 1)
                while reduced < reduced_after(cc) or (cc == 15 and reduced < REST_ADA):
                    pe.wait_ge(ada_summed, reduced + 1)
                    if reduced >= 2:
                        pe.wait_ge(row_kept, reduced - 1)
                    mm(bank(4 + reduced % 2), ones[:, :], ada_sum[:, reduced % 2, :], start=True,
                       stop=True).then_inc(ada_reduced, 1)
                    reduced += 1
            for t in range(TT):
                if t == 0:
                    pe.wait_ge(at_loaded[4], 16)
                    pe.wait_ge(at_loaded[5], 16)
                pe.wait_ge(proj_kept, 15 + t)
                for half in range(2):
                    for c in range(DC):
                        ins = mm(bank(2 * (t % 2) + half), hT[:, c, t * P:(t + 1) * P],
                                 ring[:, (4 + half) % 3, 512 * c:512 * c + 512], start=(c == 0), stop=(c == DC - 1))
                    ins.then_inc(proj_done, 1)

            def scores(qb, g, u, chunk, early=False):
                w = (qb + 1) * P
                pe.wait_ge(q_staged, g + 1)
                if not early:
                    pe.wait_ge(sig_done, g - 1)
                for n0 in range(0, w, 512):
                    n1 = min(w, n0 + 512)
                    mm(bank(2 * u, 2)[:, n0:n1], qstage[:, u, :],
                       kT[:, ds(chunk, 1), n0:n1].rearrange("p a t -> p (a t)"), start=True, stop=n1 < w)
                ins = mm(bank(2 * u, 2)[:, w - P:w], identb[:, :], maskb[:, :], start=False, stop=True)
                ins.then_inc(z_done, 1)

            def turn_probabilities(qb, g, u, first=False):
                pe.wait_ge(prob_made, g + 1)
                if first and qb:
                    pe.wait_ge(wo_scaled, qb)
                if not first or qb:
                    pe.wait_ge(probT_kept, g)
                for s in range(qb + 1):
                    ins = nc.tensor.transpose(bank(4, 2)[:, s * P:(s + 1) * P], prob[:, u, s * P:(s + 1) * P],
                                              ident[:, :])
                ins.then_inc(prob_turned, 1)

            def values(qb, g, u, chunk, pair):
                pe.wait_ge(probT_kept, g + 1)
                if u == 0 and pair is not None:
                    pe.wait_ge(o_kept, pair)
                for s in range(qb + 1):
                    ins = mm(bank(6)[:, HD * u:HD * u + HD], probT[:, u, s * P:(s + 1) * P],
                             vt[:, s, ds(chunk * P + HD * u, HD)], start=(s == 0), stop=(s == qb))
                ins.then_inc(av_done, 1)

            pe.wait_ge(proj_kept, 24)
            scores(0, 0, 0, 0, early=True)
            scores(0, 1, 1, 0, early=True)
            for qb in range(TT):
                last = qb == TT - 1
                g = 16 * qb
                scores(qb, g + 2, 0, 1)
                turn_probabilities(qb, g, 0, first=True)
                scores(qb, g + 3, 1, 1)
                turn_probabilities(qb, g + 1, 1)
                values(qb, g, 0, 0, 8 * qb if qb else None)
                with pe.Fori(1, HEADS // 2 - 1) as i:
                    gi = g + 2 * i
                    scores(qb, gi + 2, 0, i + 1)
                    turn_probabilities(qb, gi, 0)
                    values(qb, gi - 1, 1, i - 1, None)
                    scores(qb, gi + 3, 1, i + 1)
                    turn_probabilities(qb, gi + 1, 1)
                    values(qb, gi, 0, i, 8 * qb + i)
                if not last:
                    scores(qb + 1, g + 16, 0, 0)
                turn_probabilities(qb, g + 14, 0)
                values(qb, g + 13, 1, 6, None)
                if not last:
                    scores(qb + 1, g + 17, 1, 0)
                turn_probabilities(qb, g + 15, 1)
                values(qb, g + 14, 0, 7, 8 * qb + 7)
                values(qb, g + 15, 1, 7, None)
                pe.wait_ge(o_kept, 8 * qb + 8)
                if qb == 0:
                    pe.wait_ge(at_loaded[6], 16)
                    pe.wait_ge(at_loaded[7], 16)
                for half in range(2):
                    pe.wait_ge(oT_kept, 2 * qb + half) if 2 * qb + half else None
                    for c in range(4):
                        ins = nc.tensor.transpose(bank(7)[:, c * P:(c + 1) * P],
                                                  bcA[:, (4 * half + c) * P:(4 * half + c + 1) * P], ident[:, :])
                    ins.then_inc(o_turned, 1)
                pe.wait_ge(oT_kept, 2 * qb + 2)
                for half in range(2):
                    for c in range(DC):
                        ins = mm(bank(4 + half), oT[:, c, :], ring[:, half, 512 * c:512 * c + 512],
                                 start=(c == 0), stop=(c == DC - 1))
                ins.then_inc(wo_done, 1)

            def moe(l):
                pe.wait_ge(picked[l], 1)
                run = spare[:, 12 * P:12 * P + (TT + 1) * E]
                mm(bank(5)[:, 0:P], upper[:, :], spare[:, 6 * P:7 * P], start=True, stop=False)
                mm(bank(5)[:, 0:P], ones[:, :], run[:, 0:P], start=False, stop=True)
                mm(bank(5)[:, P:P + E], ones[:, :], run[:, P:P + E], start=True, stop=True).then_inc(counted[l], 1)
                pe.wait_ge(hot_made[l], 2)
                for n in range(2 * TT):
                    ins = mm(bank(6)[:, 0:TABLE], low_hot[:, n, :], high_hot[:, n, :], start=(n == 0),
                             stop=(n == 2 * TT - 1))
                ins.then_inc(table_summed[l], 1)

                def turn_rows(b, f):
                    if f == 0:
                        pe.wait_ge(x_gathered[l], 16 * b + 16)
                    for c in range(4 * f, 4 * f + 4):
                        ins = nc.tensor.transpose(bank(2, 2)[:, c * P:(c + 1) * P], xg[:, c * P:(c + 1) * P],
                                                  ident[:, :])
                    if f:
                        ins.then_inc(x_turned[l], 1)

                turn_rows(0, 0)
                turn_rows(0, 1)
                with pe.Fori(0, E // 2) as i:
                    for s in range(2):
                        wg, wu, wd = wset[s]
                        first = pe.value_load(bounds[0:1, ds(2 * i + s, 1)], min_val=0, max_val=MAXBLK)
                        end = pe.value_load(bounds[0:1, ds(2 * i + s + 1, 1)], min_val=1, max_val=MAXBLK)
                        with pe.Fori(first, end) as b:
                            pe.wait_ge(xT_kept[l], b + 1)
                            pe.wait_ge(xT_kept2[l], b + 1)
                            pe.wait_ge(w_loaded[l][s][0], 16 * i + 16)
                            for c in range(DC):
                                ins = mm(bank(0), xT[:, c, :], wg[:, F * c:F * c + F],
                                         start=(c == 0), stop=(c == DC - 1))
                            ins.then_inc(gate_done[l], 1)
                            pe.wait_ge(w_loaded[l][s][1], 16 * i + 16)
                            for f in range(2):
                                for c in range(DC):
                                    ins = mm(bank((1, 7)[f])[:, 0:256], xT[:, c, :],
                                             wu[:, F * c + 256 * f:F * c + 256 * f + 256],
                                             start=(c == 0), stop=(c == DC - 1))
                                ins.then_inc(up_done[l], 1)
                            for f in range(2):
                                pe.wait_ge(ha_made[l], 2 * b + f + 1)
                                for c in range(2):
                                    at = 256 * f + P * c
                                    ins = nc.tensor.transpose(bank((4, 0)[f])[:, c * P:(c + 1) * P], ha[:, at:at + P],
                                                              ident[:, :])
                                ins.then_inc(ha_turned[l], 1)
                                turn_rows(b + 1, f)
                            pe.wait_ge(w_loaded[l][s][2], 16 * i + 16)
                            pe.wait_ge(haT_kept[l], 2 * b + 2)
                            for half in range(2):
                                for c in range(F // P):
                                    ins = mm(bank(5 + half), haT[:, c * P:(c + 1) * P],
                                             wd[:, D * c + 512 * half:D * c + 512 * half + 512],
                                             start=(c == 0), stop=(c == F // P - 1))
                                ins.then_inc(down_done[l], 1)

            for t in range(TT):
                turn(1, t)
                if t:
                    logits(1, t - 1)
            logits(1, TT - 1)
            moe(0)
            for t in range(TT):
                turn(2, t)
            turned(2, TT - 1)
            for c in range(DC):
                g = 4 * (c % 2)
                if c % 4 == 0:
                    pe.wait_ge(cv_loaded[c // 2], 16)
                    pe.wait_ge(cv_loaded[c // 2 + 1], 16)
                if c >= 2:
                    pe.wait_ge(u_done, c - 1)
                for part in range(2):
                    slot = (2 * (c // 4) + part) % 3
                    for half in range(2):
                        for k in range(DC):
                            ins = mm(bank(g + 2 * part + half),
                                     ring[:, slot, 512 * k + P * (c % 4):512 * k + P * (c % 4) + P],
                                     hT[:, k, 512 * half:512 * half + 512], start=(k == 0), stop=(k == DC - 1))
                ins.then_inc(in_done, 1)
            pe.wait_ge(u_done, DC)
            for c in range(DC):
                pe.wait_ge(conv_done, c + 1)
                for half in range(2):
                    ins = mm(bank(half), ones[:, :], cv[:, c, 512 * half:512 * half + 512],
                             start=(c == 0), stop=(c == DC - 1), skip_group_check=True)
            ins.then_inc(mean_done, 1)
            for c in range(DC):
                pe.wait_ge(squared, c + 1)
                for half in range(2):
                    ins = mm(bank(2 + half), ones[:, :], usig[:, c % 2, 512 * half:512 * half + 512],
                             start=(c == 0), stop=(c == DC - 1), skip_group_check=True)
                ins.then_inc(var_done, 1)
            pe.wait_ge(ln_done, DC)
            pe.wait_ge(cv_loaded[4], 16)
            pe.wait_ge(cv_loaded[5], 16)
            for t in range(TT):
                for half in range(2):
                    n = 2 * t + half
                    if n >= 3:
                        pe.wait_ge(out_used, n - 2)
                    for c in range(DC):
                        ins = mm(bank(5 + n % 3), hT[:, c, t * P:(t + 1) * P],
                                 ring[:, (4 + half) % 3, 512 * c:512 * c + 512], start=(c == 0), stop=(c == DC - 1))
                    ins.then_inc(out_done, 1)
                if t >= 1:
                    turn(3, t - 1)
                if t >= 2:
                    logits(3, t - 2)
            turn(3, TT - 1)
            logits(3, TT - 2)
            logits(3, TT - 1)
            moe(1)


def kernel(**inputs):
    import numpy as np
    import concourse.bacc as bacc
    from concourse.bass_utils import run_bass_kernel_spmd

    a = {k: np.asarray(v) for k, v in inputs.items()}

    def pieces(w, k, order=None):
        w = w.reshape(-1, k, P, w.shape[-1] // 512, 512).transpose(0, 3, 2, 1, 4)
        w = w.reshape(-1, P, k * 512)
        return np.ascontiguousarray(w if order is None else w[order])

    def col(v):
        return v.reshape(-1, P).T

    def rows(w, k):
        return np.ascontiguousarray(w.reshape(-1, k, P, w.shape[-1]).transpose(0, 2, 1, 3)).reshape(-1, P, k * w.shape[-1])

    dw = a["cv_w_dw"][0].reshape(CW, DC, P).transpose(2, 1, 0).reshape(P, DC * CW)
    data = {
        "x": a["x"].reshape(T, D),
        "c_col": col(a["c"]),
        "b_ada": a["b_ada"].reshape(1, -1),
        "final_g": a["final_g"],
        "vec_cols": np.concatenate([col(a["c"]), col(a["cv_b_in"]), dw, col(a["cv_b_dw"]), col(a["cv_ln_g"]),
                                    col(a["cv_ln_b"])]
                                   + [col(a[f"norm{k}_g"][l]) for l in range(2) for k in (1, 2)], axis=1),
        "b_out": a["cv_b_out"].reshape(D),
        "b_router": a["b_router"],
        "w_router": a["w_router"].reshape(DC, P, E).transpose(1, 0, 2),
        "w_ada": pieces(a["w_ada"], DC),
        "w_qkv": pieces(a["sb_w_qkv"], DC),
        "w_o": pieces(a["sb_w_o"], DC),
        "w_in": pieces(a["cv_w_in"], DC, [0, 2, 1, 3]),
        "w_out": pieces(a["cv_w_out"], DC),
        "w_gate": rows(a["moe_w_gate"], DC),
        "w_up": rows(a["moe_w_up"], DC),
        "w_down": rows(a["moe_w_down"], F // P),
    }
    nc = bacc.Bacc("TRN2", target_bir_lowering=False, num_devices=1)
    arrays, args = {}, []
    for name, v in data.items():
        v = np.ascontiguousarray(v)
        arrays[f"in_{name}"] = v
        args.append(nc.dram_tensor(f"in_{name}", v.shape, mybir.dt.from_np(v.dtype), kind="ExternalInput").ap())
    out = nc.dram_tensor("out_x", (T, D), mybir.dt.float32, kind="ExternalOutput").ap()
    trunk(nc, *args, out)
    r = run_bass_kernel_spmd(nc, [arrays], core_ids=[0])
    return r.results[0]["out_x"].reshape(1, T, D)
```

```python
from contextlib import ExitStack

import concourse.bass as bass
from concourse import mybir

P = 128
T, D, F, E = 1024, 1024, 512, 16
HEADS, HD = 16, 64
TT, DC = T // P, D // P
GROUPS, EPG = 4, 4
CW = 31
EPS = 1e-6
PIECE = DC * 512
ADA = 12
FIRST_ADA = 4
REST_ADA = 2 * ADA - FIRST_ADA
MAXBLK = 32
TABLE = MAXBLK + 2
ADD_TAPS = [10] * (DC - 2) + [9] * 2
PE_TAPS = [0] * (DC - 2) + [7] * 2


def trunk(nc, x, c_col, b_ada, final_g, vec_cols, b_out, b_router, w_router, w_ada, w_qkv, w_o, w_in, w_out,
          w_gate, w_up, w_down, out):
    f32, i32 = mybir.dt.float32, mybir.dt.int32
    ALU, ACT, AX = mybir.AluOpType, mybir.ActivationFunctionType, mybir.AxisListType
    ds = bass.ds

    mod_dram = nc.dram_tensor("mod_rows", (2 * 6 * D,), f32, kind="Internal").ap()
    h_dram = [nc.dram_tensor(f"h_rows{l}", (T, D), f32, kind="Internal").ap() for l in range(2)]
    y_dram = [nc.dram_tensor(f"expert_rows{l}", (MAXBLK * P, D), f32, kind="Internal").ap() for l in range(2)]

    ctx = ExitStack()
    with ctx:
        def sb(name, shape, dt=f32):
            return ctx.enter_context(nc.sbuf_tensor(name, shape, dt))

        def sem(name):
            return ctx.enter_context(nc.semaphore(name))

        xq = sb("xq", [P, TT, DC, P])
        kv = sb("kv", [P, 4 * PIECE])
        hT = sb("hT", [P, DC, T])
        ring = sb("ring", [P, 3, PIECE])
        bcA, bcB, bcC = sb("bcA", [P, D]), sb("bcB", [P, D]), sb("bcC", [P, D])
        pbuf = sb("pbuf", [P, 2, D + 2])
        oT = sb("oT", [P, DC, P])
        ident, ones, upper = sb("ident", [P, P]), sb("ones", [P, P]), sb("upper", [P, P])
        identb, maskb = sb("identb", [P, P], mybir.dt.bfloat16), sb("maskb", [P, P], mybir.dt.bfloat16)
        pace, eps = sb("pace", [P, 2]), sb("eps", [P, 1])
        half_ones = sb("half_ones", [P, 2, P])
        qstage = sb("qstage", [P, 2, P])
        cols = sb("cols", [P, 296 + 4 * DC])
        modc = sb("modc", [P, 4, 2, DC])
        cond = sb("cond", [P, DC])
        wr = sb("wr", [P, DC, E])
        brt = sb("brt", [P, E])
        ss, rstd = sb("ss", [P, TT]), sb("rstd", [P, TT])
        tokid, tile_first = sb("tokid", [P, TT]), sb("tile_first", [P, TT])
        pref_e, pref_g = sb("pref_e", [P, TT, E]), sb("pref_g", [P, TT, GROUPS])
        dest = sb("dest", [P, 2, TT], i32)
        wts = sb("wts", [P, 2, TT])
        bounds = sb("bounds", [1, E + 1], i32)
        slot_i = sb("slot_i", [P, 2, 2 * TT], i32)
        slot_tok = sb("slot_tok", [P, TABLE], i32)
        idx_now = sb("idx_now", [P, 1], i32)

        iota_i = qstage[:, 0, :].bitcast(i32)
        lane = half_ones[:, 0, :]
        ccol = cols[:, 0:8]
        b_in_c, w_dw_c = cols[:, 8:24], cols[:, 24:24 + 248].rearrange("p (c k) -> p c k", c=DC)
        b_dw_c, ln_g_c, ln_b_c = cols[:, 272:280], cols[:, 280:288], cols[:, 288:296]
        norm_c = cols[:, 296:296 + 4 * DC]
        hbuf = [pbuf[:, 0, 0:D], pbuf[:, 1, 0:D], bcA[:, :], bcB[:, :]]


        def hrow(n, t):
            return kv[:, D * t:D * (t + 1)] if n == 1 else hbuf[t % 4]

        vslot = [kv[:, (2 + u) * PIECE:(3 + u) * PIECE] for u in range(2)]
        bias = oT[:, :, :].rearrange("p c t -> p (c t)").rearrange("p (u n) -> p u n", u=2)
        ada_sum = pbuf[:, :, 0:512]
        ada_out = bcA[:, :].rearrange("p (u n) -> p u n", u=2)
        kT = kv[:, 0:2 * PIECE].rearrange("p (c t) -> p c t", c=DC)
        vt = kv[:, 2 * PIECE:4 * PIECE].rearrange("p (s f) -> p s f", s=TT)
        beta, omega, prob, probT = hT[:, 0:2, :], hT[:, 2:4, :], hT[:, 4:6, :], hT[:, 6:8, :]
        cv = kT
        UW = T + CW - 1
        upad = kv[:, 2 * PIECE:2 * PIECE + 2 * UW].rearrange("p (b t) -> p b t", b=2)
        o_ = 2 * PIECE + 2 * UW
        usig = kv[:, o_:o_ + 2 * T].rearrange("p (b t) -> p b t", b=2)
        tapp = kv[:, o_ + 2 * T:o_ + 4 * T].rearrange("p (b t) -> p b t", b=2)
        acc2 = kv[:, o_ + 4 * T:o_ + 5 * T]
        scT = oT[0:E, :, :].rearrange("p c t -> p (c t)")
        hflat = hT[:, :, :].rearrange("p c t -> p (c t)")
        xg, xT = hflat[:, 0:1024], hflat[:, 1024:2048].rearrange("p (c t) -> p c t", c=DC)
        sg, ha, haT = hflat[:, 2048:2560], hflat[:, 2560:3072], hflat[:, 3072:3584]
        yo = hflat[:, 3584:4608]
        wset = [[ring[:, k, :] for k in range(3)], [kv[:, k * PIECE:(k + 1) * PIECE] for k in range(3)]]
        spare = kv[:, 3 * PIECE:4 * PIECE]
        ygat = [kv[:, 2 * D * b:2 * D * (b + 1)].rearrange("p (k d) -> p k d", k=2) for b in range(4)]
        hots = hflat[:, 4608:8192].bitcast(mybir.dt.bfloat16)
        low_hot = hots[:, 0:2 * TT * P].rearrange("p (n q) -> p n q", q=P)
        high_hot, high_row, high_tile = (
            hots[:, 2 * TT * (P + k * TABLE):2 * TT * (P + (k + 1) * TABLE)].rearrange("p (n b) -> p n b", b=TABLE)
            for k in range(3))

        def tmp(n, w=E):
            return spare[:, n * P:n * P + TT * w].rearrange("p (t e) -> p t e", t=TT)

        ps = ctx.enter_context(nc.psum_tensor("ps", [P, 8 * 512], f32))

        def bank(b, n=1):
            return ps[:, 512 * b:512 * (b + n)]

        const_made = sem("const_made")
        x_loaded, cols_loaded = [sem(f"x_loaded{h}") for h in range(2)], sem("cols_loaded")
        cond_made = sem("cond_made")
        zeros_made = sem("zeros_made")
        ada_first = [sem(f"ada_first{n}") for n in range(FIRST_ADA)]
        ada_loaded = [sem(f"ada_loaded{u}") for u in range(2)]
        bias_loaded = [sem(f"bias_loaded{u}") for u in range(2)]
        row_stored = [sem(f"row_stored{u}") for u in range(2)]
        ada_used, ada_row, row_turned = sem("ada_used"), sem("ada_row"), sem("row_turned")
        bias_zeroed, ada_step, ada_summed, ada_reduced, row_kept = (
            sem("bias_zeroed"), sem("ada_step"), sem("ada_summed"), sem("ada_reduced"), sem("row_kept"))
        bc_loaded, gate_loaded, modc_loaded, modc_made = (sem("bc_loaded"), sem("gate_loaded"), sem("modc_loaded"),
                                                          sem("modc_made"))
        root_done = sem("root_done")
        sq_done, h_made, h_turned, h_kept, h_kept2 = (sem("sq_done"), sem("h_made"), sem("h_turned"), sem("h_kept"),
                                                      sem("h_kept2"))
        h_stored = [sem(f"h_stored{b}") for b in range(4)]
        at_loaded = [sem(f"at_loaded{j}") for j in range(8)]
        proj_done, proj_kept = sem("proj_done"), sem("proj_kept")
        q_staged, z_done, sig_done, omega_done, scanned = sem("q_staged"), sem("z_done"), sem("sig_done"), sem("omega_done"), sem("scanned")
        prob_made, prob_turned, probT_kept, av_done, o_kept = (sem("prob_made"), sem("prob_turned"),
                                                               sem("probT_kept"), sem("av_done"), sem("o_kept"))
        o_turned, oT_kept, wo_done, wo_scaled, x_again, x_made = (sem("o_turned"), sem("oT_kept"), sem("wo_done"),
                                                                  sem("wo_scaled"), sem("x_again"), sem("x_made"))
        cv_loaded = [sem(f"cv_loaded{j}") for j in range(6)]
        values_done, var_kept = sem("values_done"), sem("var_kept")
        in_done, usig_done, u_done, tap_made, tap_added, conv_done = (
            sem("in_done"), sem("usig_done"), sem("u_done"), sem("tap_made"), sem("tap_added"), sem("conv_done"))
        ln_summed, cv_moved, squared, ln_root, ln_done = (
            sem("ln_summed"), sem("cv_moved"), sem("squared"), sem("ln_root"),
            sem("ln_done"))
        diag_made, taps_summed = sem("diag_made"), sem("taps_summed")
        out_done, out_used = sem("out_done"), sem("out_used")
        both = lambda name: [sem(f"{name}{l}") for l in range(2)]
        scT_made = both("scT_made")
        logits_done, score_done, picked, counted, hot_made = (
            both("logits_done"), both("score_done"), both("picked"), both("counted"), both("hot_made"))
        bounds_made, table_summed, table_made = both("bounds_made"), both("table_summed"), both("table_made")
        w_loaded = [[[sem(f"w_loaded{l}{s}{k}") for k in range(3)] for s in range(2)] for l in range(2)]
        x_gathered, x_turned, xT_kept, xT_kept2 = (
            both("x_gathered"), both("x_turned"), both("xT_kept"), both("xT_kept2"))
        gate_done, up_done, silu_done, ha_made, ha_turned, haT_kept = (
            both("gate_done"), both("up_done"), both("silu_done"), both("ha_made"), both("ha_turned"), both("haT_kept"))
        down_done, y_kept = both("down_done"), both("y_kept")
        stored = both("stored")
        y_gathered = [[sem(f"y_gathered{l}{b}") for b in range(4)] for l in range(2)]
        x_added = both("x_added")
        dve_step = sem("dve_step")
        final_made, out_stored = sem("final_made"), [sem(f"out_stored{b}") for b in range(2)]

        block = ctx.enter_context(nc.Block())

        MOD = [(0, 0, 1, 2), (0, 3, 4, 5), (1, 0, 1, 2), (1, 3, 4, 5)]

        def qk_bank(n):
            return 0 if n % 2 else 6

        def made_before(c):
            return sum(ADD_TAPS[:c])

        def added_before(c):
            return sum(ADD_TAPS[:c]) - c

        diag_chunk = [c for c in range(DC) for _ in range(PE_TAPS[c])]
        diag_tap = [CW - PE_TAPS[c] + k for c in range(DC) for k in range(PE_TAPS[c])]

        def diag(n):
            return hbuf[(2, 3, 0)[n // 8]][:, n % 8 * P:(n % 8 + 1) * P]

        def taps_bank(c):
            return 4 if c == DC - 2 else 0

        def reduced_after(cc):
            return 0 if cc < 1 else min(REST_ADA, (cc - 1) * REST_ADA // 13)

        def mod_row(l, j):
            return mod_dram[(6 * l + j) * D:(6 * l + j + 1) * D].partition_broadcast(P)

        def mod_col(l, j):
            return mod_dram[(6 * l + j) * D:(6 * l + j + 1) * D].rearrange("(c p) -> p c", p=P)

        def xtile(t):
            return xq[:, t, :, :].rearrange("p c j -> p (c j)")

        @block.sync
        def _(sp):
            sp.dma_start(cols[:, :], vec_cols).then_inc(cols_loaded, 16)
            sp.dma_start(kv[0:1, 0:2 * D], b_ada[:, 0:2 * D]).then_inc(cols_loaded, 16)
            sp.dma_start(wr[:, :, :], w_router).then_inc(cols_loaded, 16)
            sp.dma_start(brt[:, :], b_router.partition_broadcast(P)).then_inc(cols_loaded, 16)

            def load_x(h):
                tiles = slice(TT // 2 * h, TT // 2 * (h + 1))
                sp.dma_start(xq[:, tiles, :, :].rearrange("p t c j -> p t (c j)"),
                             x[P * TT // 2 * h:P * TT // 2 * (h + 1), :].rearrange("(t p) d -> p t d", p=P)
                             ).then_inc(x_loaded[h], 16)

            for n in range(FIRST_ADA):
                if n >= 3:
                    load_x(0)
                    sp.wait_ge(ada_used, n - 2)
                sp.dma_start(ring[:, (n + 2) % 3, :], w_ada[n]).then_inc(ada_first[n], 16)
            load_x(1)
            for j in range(8):
                if j < 3:
                    sp.wait_ge(ada_used, (2, 3, 4)[j])
                else:
                    sp.wait_ge(proj_done, (4, 8, 12, 16, 32)[j - 3])
                sp.dma_start(ring[:, j % 3, :], w_qkv[j] if j < 6 else w_o[j - 6]).then_inc(at_loaded[j], 16)
                if j == 2:
                    for u in range(2):
                        sp.dma_start(vslot[u], w_ada[FIRST_ADA + u]).then_inc(ada_loaded[u], 16)
                if 2 <= j <= 4:
                    with sp.Fori(*((1, 4), (4, 7), (7, REST_ADA // 2))[j - 2]) as i:
                        for u in range(2):
                            sp.wait_ge(ada_summed, 2 * i + u - 1)
                            sp.dma_start(vslot[u], w_ada[ds(2 * i + u + FIRST_ADA, 1)].rearrange("a p n -> (a p) n")
                                         ).then_inc(ada_loaded[u], 16)
            for l in range(2):
                sp.wait_ge(stored[l], 16)
            weights = (w_gate, w_up, w_down)

            def first_expert(l, s, k):
                sp.dma_start(wset[s][k], weights[k][l * E + s]).then_inc(w_loaded[l][s][k], 16)

            def experts(l):
                sp.wait_ge(bounds_made[l], 1)
                with sp.Fori(1, E // 2) as i:
                    for s in range(2):
                        ends = sp.value_load(bounds[0:1, ds(2 * i + s - 1, 1)], min_val=1, max_val=MAXBLK)
                        for k, w in enumerate(weights):
                            if k == 0:
                                sp.wait_ge(gate_done[l], ends)
                            elif k == 1:
                                sp.wait_ge(up_done[l], 2 * ends)
                            else:
                                sp.wait_ge(down_done[l], 2 * ends)
                            sp.dma_start(wset[s][k], w[ds(2 * i + s + l * E, 1)].rearrange("a p n -> (a p) n")
                                         ).then_inc(w_loaded[l][s][k], 16)
                ends = sp.value_load(bounds[0:1, E - 1:E], min_val=1, max_val=MAXBLK)
                sp.wait_ge(down_done[l], 2 * ends)

            first_expert(0, 0, 2)
            sp.wait_ge(wo_done, TT)
            for k in range(2):
                first_expert(0, 0, k)
            sp.wait_ge(h_turned, 2 * TT)
            for b in range(4):
                sp.wait_ge(h_stored[b], 16 * TT // 4)
            for k in range(3):
                first_expert(0, 1, k)
            experts(0)
            for j in range(6):
                if j >= 3:
                    sp.wait_ge((values_done, in_done, values_done)[j - 3], (4, 4, 8)[j - 3])
                sp.dma_start(ring[:, j % 3, :], w_in[j] if j < 4 else w_out[j - 4]).then_inc(cv_loaded[j], 16)
            sp.wait_ge(in_done, DC)
            first_expert(1, 0, 0)
            sp.wait_ge(ln_done, 2 * DC)
            for k in range(3):
                first_expert(1, 1, k)
            sp.wait_ge(out_done, 2 * TT)
            for k in range(1, 3):
                first_expert(1, 0, k)
            experts(1)
            for t in range(TT):
                sp.wait_ge(final_made, t + 1)
                sp.dma_start(out[t * P:(t + 1) * P, :], pbuf[:, t % 2, 0:D]).then_inc(out_stored[t % 2], 16)
            for b in range(2):
                sp.wait_ge(out_stored[b], 16 * TT // 2)

        @block.gpsimd
        def _(pool):
            nc.gpsimd.memset(ident[:, :], 0.0)
            nc.gpsimd.memset(upper[:, :], 1.0)
            nc.gpsimd.memset(ones[:, :], 1.0)
            nc.gpsimd.memset(maskb[:, :], 0.0)
            nc.gpsimd.memset(eps[:, :], EPS)
            nc.gpsimd.memset(identb[:, :], 0.0)
            nc.gpsimd.memset(pbuf[:, :, D:D + 2], 1.0)
            nc.gpsimd.memset(half_ones[:, :, :], 1.0).then_inc(const_made, 1)
            pool.wait_ge(const_made, 1)
            nc.gpsimd.affine_select(out=ident[:, :], in_=ident[:, :], compare_op=ALU.not_equal, fill=1.0, base=0,
                                    pattern=[[-1, P]], channel_multiplier=1)
            nc.gpsimd.affine_select(out=half_ones[:, 0, :], in_=half_ones[:, 0, :], compare_op=ALU.is_gt, fill=0.0,
                                    base=HD, pattern=[[0, P]], channel_multiplier=-1)
            nc.gpsimd.affine_select(out=half_ones[:, 1, :], in_=half_ones[:, 1, :], compare_op=ALU.is_ge, fill=0.0,
                                    base=-HD, pattern=[[0, P]], channel_multiplier=1)
            nc.gpsimd.affine_select(out=maskb[:, :], in_=maskb[:, :], compare_op=ALU.is_gt, fill=-1e30, base=0,
                                    pattern=[[-1, P]], channel_multiplier=1)
            nc.gpsimd.affine_select(out=identb[:, :], in_=identb[:, :], compare_op=ALU.not_equal, fill=1.0, base=0,
                                    pattern=[[-1, P]], channel_multiplier=1)
            nc.gpsimd.affine_select(out=upper[:, :], in_=upper[:, :], compare_op=ALU.is_gt, fill=0.0, base=0,
                                    pattern=[[1, P]], channel_multiplier=-1).then_inc(const_made, 1)
            for n, (pattern, base, mul, width) in enumerate((([[P, TT]], 0, 1, TT), ([[0, TT], [-1, GROUPS]], GROUPS, 0,
                                                              TT * GROUPS), ([[0, TT], [-1, E]], E, 0, TT * E))):
                if n:
                    pool.wait_ge(dve_step, n)
                nc.gpsimd.iota(iota_i[:, 0:width], pattern=pattern, base=base, channel_multiplier=mul).then_inc(
                    const_made, 1)

            def load_modc(n):
                l, shift, scale, gate = MOD[n]
                with nc.allow_non_contiguous_dma("a vector by its chunks, to columns"):
                    pool.dma_start(modc[:, n, 0, :], mod_col(l, shift)).then_inc(modc_loaded, 16)
                    pool.dma_start(modc[:, n, 1, :], mod_col(l, scale)).then_inc(modc_loaded, 16)

            def load_gate(l, j):
                pool.dma_start(bcC[:, :], mod_row(l, j)).then_inc(gate_loaded, 16)

            def store_h(n, t):
                pool.wait_ge(h_made, TT * n + t + 1)
                pool.dma_start(h_dram[n // 2][t * P:(t + 1) * P, :], hrow(n, t)).then_inc(h_stored[t % 4], 16)

            pool.wait_ge(bias_zeroed, 1)
            for n in range(REST_ADA + 2):
                u = n % 2
                if n < REST_ADA:
                    if n >= 2:
                        pool.wait_ge(ada_summed, n - 1)
                    pool.dma_start(bias[0:1, u, :], b_ada[:, 512 * (FIRST_ADA + n):512 * (FIRST_ADA + n + 1)]
                                   ).then_inc(bias_loaded[u], 16)
                if n >= 2:
                    m = FIRST_ADA + n - 2
                    pool.wait_ge(row_kept, n - 1)
                    pool.dma_start(mod_dram[512 * m:512 * (m + 1)].unsqueeze(0), ada_out[0:1, u, :]
                                   ).then_inc(row_stored[u], 16)
            for u in range(2):
                pool.wait_ge(row_stored[u], 16 * REST_ADA // 2)
            for n in range(1, 4):
                load_modc(n)
            load_gate(0, 2)

            def stage(qb, chunk, u):
                nc.gpsimd.tensor_tensor(qstage[:, u, :], xq[:, qb, ds(chunk, 1), :].rearrange("p a t -> p (a t)"),
                                        half_ones[:, u, :], ALU.mult).then_inc(q_staged, 1)

            pool.wait_ge(proj_kept, 16)
            stage(0, 0, 0)
            stage(0, 0, 1)
            for qb in range(TT):
                with pool.Fori(0, HEADS // 2 - 1) as i:
                    for u in range(2):
                        g = 16 * qb + 2 * i + u
                        pool.wait_ge(z_done, g + 1)
                        nc.gpsimd.tensor_tensor(pace[:, u:u + 1], ones[:, 0:1], ones[:, 0:1], ALU.mult)
                        stage(qb, i + 1, u)
                if qb:
                    pool.wait_ge(x_made, qb)
                pool.dma_start(bcB[:, :], x[qb * P:(qb + 1) * P, :]).then_inc(x_again, 16)
                if qb in (3, 4):
                    if qb == 3:
                        pool.wait_ge(zeros_made, 1)
                    pool.dma_start(y_dram[qb - 3][E * P:, :].rearrange("(b p) d -> p b d", p=P),
                                   ring[:, 2, 0:D].unsqueeze(1).to_broadcast([P, MAXBLK - E, D])).then_inc(
                                       stored[qb - 3], 16)
                for u in range(2):
                    if qb < TT - 1:
                        pool.wait_ge(z_done, 16 * qb + 14 + u + 1)
                        stage(qb + 1, 0, u)

            def moe(l):
                pool.wait_ge(table_made[l], 1)
                for b in range(4):
                    pool.wait_ge(h_stored[b], 16 * TT // 4 * (l + 1))
                if l:
                    pool.dma_start(bcA[:, :], final_g.partition_broadcast(P)).then_inc(bc_loaded, 16)

                def gather(b):
                    nc.gpsimd.tensor_copy(idx_now[:, :], slot_tok[:, ds(b, 1)])
                    pool.drain()
                    pool.indirect_dma_start(
                        out=xg, out_offset=None, in_=h_dram[l],
                        in_offset=bass.IndirectOffsetOnAxis(ap=idx_now[:, 0:1], axis=0)).then_inc(x_gathered[l], 16)

                gather(0)
                pool.wait_ge(x_turned[l], 1)
                gather(1)
                blocks = pool.value_load(bounds[0:1, E:E + 1], min_val=1, max_val=MAXBLK)
                with pool.Fori(0, blocks) as b:
                    pool.wait_ge(x_turned[l], b + 2)
                    gather(b + 2)
                    pool.wait_ge(y_kept[l], 2 * b + 2)
                    pool.dma_start(y_dram[l][ds(b * P, P), :], yo).then_inc(stored[l], 16)
                    pool.wait_ge(x_gathered[l], 16 * b + 48)
                    pool.wait_ge(stored[l], 16 * b + 32)
                for t in range(TT):
                    if t >= 4:
                        pool.wait_ge(x_added[l], t - 3)
                    for k in range(2):
                        pool.indirect_dma_start(
                            out=ygat[t % 4][:, k, :], out_offset=None, in_=y_dram[l],
                            in_offset=bass.IndirectOffsetOnAxis(ap=dest[:, k, t:t + 1], axis=0)
                        ).then_inc(y_gathered[l][t % 4], 16)

            for t in range(TT - 1):
                store_h(1, t)
            pool.wait_ge(x_made, TT)
            nc.gpsimd.iota(iota_i, pattern=[[1, P]], base=0, channel_multiplier=0).then_inc(const_made, 1)
            store_h(1, TT - 1)
            load_gate(0, 5)
            moe(0)
            load_gate(1, 2)
            for c in range(DC):
                for j in range(1, ADD_TAPS[c]):
                    pool.wait_ge(tap_made, made_before(c) + j + 1)
                    nc.gpsimd.tensor_tensor(acc2, acc2, tapp[:, j % 2, :], ALU.add).then_inc(tap_added, 1)
                    if j < ADD_TAPS[c] - 1:
                        pool.wait_ge(tap_added, added_before(c) + j)
            pool.wait_ge(tap_added, added_before(DC))
            pool.dma_start(tapp[:, 0, :], b_out.partition_broadcast(P)).then_inc(bc_loaded, 16)
            for t in range(TT):
                store_h(3, t)
            pool.wait_ge(out_used, 2 * TT)
            load_gate(1, 5)
            moe(1)

        @block.scalar
        def _(act):
            act.wait_ge(cols_loaded, 64)
            nc.scalar.activation(cond[:, :], ccol, ACT.Silu).then_inc(cond_made, 1)

            def square(n, t):
                nc.scalar.activation(oT[:, :, :].rearrange("p c t -> p (c t)"), xtile(t), ACT.Square,
                                     accum_out=ss[:, t:t + 1]).then_inc(sq_done, 1)
                act.wait_ge(sq_done, TT * n + t + 1)

            def roots(n, t, tiles=1):
                nc.scalar.activation(rstd[:, t:t + tiles], ss[:, t:t + tiles], ACT.Sqrt, bias=eps[:, :],
                                     scale=1.0 / D).then_inc(root_done, tiles)

            def norm_keep(n, t):
                act.wait_ge(h_turned, TT * n + t + 1)
                for c in range(4):
                    ins = nc.scalar.activation(hT[:, c, t * P:(t + 1) * P], bank(2 * (t % 2))[:, c * P:(c + 1) * P],
                                               ACT.Identity, bias=modc[:, n, 0, c:c + 1],
                                               scale=modc[:, n, 1, c:c + 1])
                ins.then_inc(h_kept, 1)

            def keep_scores(l, half):
                act.wait_ge(logits_done[l], TT // 2 * (half + 1))
                nc.scalar.activation(scT[:, 512 * half:512 * half + 512], bank(4 + half)[0:E, :],
                                     ACT.Sigmoid).then_inc(scT_made[l], 1)

            def keep_row(n):
                if n >= 2:
                    act.wait_ge(row_stored[n % 2], 16 * (n // 2))
                act.wait_ge(ada_reduced, n + 1)
                nc.scalar.activation(ada_out[0:1, n % 2, :], bank(4 + n % 2)[0:1, :], ACT.Copy).then_inc(row_kept, 1)

            act.wait_ge(const_made, 2)
            for h in range(2):
                act.wait_ge(x_loaded[h], 16)
                for t in range(TT // 2 * h, TT // 2 * (h + 1)):
                    square(0, t)
                roots(0, TT // 2 * h, TT // 2)
            act.wait_ge(modc_made, 1)
            for t in range(TT):
                norm_keep(0, t)
            kept = 0
            for cc in range(16):
                while kept < reduced_after(cc - 1):
                    keep_row(kept)
                    kept += 1
                act.wait_ge(proj_done, cc + 1)
                src = bank(qk_bank(cc), 2)
                if cc < 8:
                    nc.scalar.activation(xq[:, :, cc, :], src.rearrange("p (t j) -> p t j", t=TT),
                                         ACT.Copy).then_inc(proj_kept, 1)
                else:
                    nc.scalar.activation(kT[:, cc - 8, :], src, ACT.Copy).then_inc(proj_kept, 1)
            while kept < REST_ADA:
                keep_row(kept)
                kept += 1
            act.wait_ge(ada_summed, REST_ADA)
            for t in range(TT):
                act.wait_ge(proj_done, 16 + 2 * (t + 1))
                nc.scalar.activation(vt[:, t, :], bank(qk_bank(t), 2), ACT.Copy).then_inc(proj_kept, 1)

            def sigmoids(qb, g, u, early=False):
                w = (qb + 1) * P
                act.wait_ge(z_done, g + 1)
                if not early:
                    act.wait_ge(scanned, g - 1)
                nc.scalar.activation(omega[:, u, 0:w], bank(2 * u, 2)[:, 0:w], ACT.Sigmoid,
                                     scale=-HD ** -0.5).then_inc(omega_done, 1)
                if not early:
                    act.wait_ge(prob_made, g - 1)
                nc.scalar.activation(beta[:, u, 0:w], bank(2 * u, 2)[:, 0:w], ACT.Sigmoid,
                                     scale=HD ** -0.5).then_inc(sig_done, 1)

            def keep_turned(qb, g, u):
                w = (qb + 1) * P
                act.wait_ge(prob_turned, g + 1)
                nc.scalar.activation(probT[:, u, 0:w], bank(4, 2)[:, 0:w], ACT.Copy).then_inc(probT_kept, 1)

            sigmoids(0, 0, 0, early=True)
            sigmoids(0, 1, 1, early=True)
            for qb in range(TT):
                with act.Fori(0, HEADS // 2 - 1) as i:
                    for u in range(2):
                        g = 16 * qb + 2 * i + u
                        sigmoids(qb, g + 2, u)
                        keep_turned(qb, g, u)
                if qb:
                    act.wait_ge(x_made, qb)
                    square(1, qb - 1)
                for u in range(2):
                    g = 16 * qb + 14 + u
                    if qb < TT - 1:
                        sigmoids(qb + 1, g + 2, u)
                    keep_turned(qb, g, u)
                for half in range(2):
                    act.wait_ge(o_turned, 2 * qb + half + 1)
                    nc.scalar.activation(oT[:, 4 * half:4 * half + 4, :],
                                         bank(7 - half).rearrange("p (c t) -> p c t", c=4), ACT.Copy).then_inc(oT_kept, 1)
            roots(1, 0, TT - 1)

            def moe(l):
                keep_scores(l, 1)

                def keep(b):
                    act.wait_ge(x_turned[l], b + 1)
                    for c in range(4):
                        ins = nc.scalar.activation(xT[:, c, :], bank(2)[:, c * P:(c + 1) * P], ACT.Identity,
                                                   bias=modc[:, 2 * l + 1, 0, c:c + 1],
                                                   scale=modc[:, 2 * l + 1, 1, c:c + 1])
                    ins.then_inc(xT_kept[l], 1)

                keep(0)
                blocks = act.value_load(bounds[0:1, E:E + 1], min_val=1, max_val=MAXBLK)
                with act.Fori(0, blocks) as b:
                    act.wait_ge(gate_done[l], b + 1)
                    nc.scalar.activation(sg, bank(0), ACT.Silu).then_inc(silu_done[l], 1)
                    act.wait_ge(up_done[l], 2 * b + 2)
                    keep(b + 1)

            act.wait_ge(x_made, TT)
            square(1, TT - 1)
            roots(1, TT - 1)
            act.wait_ge(modc_made, 4)
            for t in range(TT):
                norm_keep(1, t)
                if t == TT - 2:
                    keep_scores(0, 0)
            moe(0)
            for t in range(TT + 2):
                if t < TT:
                    act.wait_ge(x_added[0], t + 1)
                    square(2, t)
                    roots(2, t)
                if t >= 2:
                    norm_keep(2, t - 2)
            for c in range(DC):
                g = 4 * ((c + 1) % 2)
                act.wait_ge(in_done, c + 1)
                nc.scalar.activation(usig[:, c % 2, :], bank(g + 2, 2), ACT.Sigmoid,
                                     bias=b_in_c[:, 8 + c:9 + c]).then_inc(usig_done, 1)
                act.wait_ge(u_done, c + 1)
                if c == 1:
                    for n in range(sum(PE_TAPS)):
                        ins = nc.scalar.activation(diag(n), ident[:, :], ACT.Copy, scale=w_dw_c[:, diag_chunk[n],
                                                   diag_tap[n]:diag_tap[n] + 1])
                    ins.then_inc(diag_made, 1)
                for j in range(ADD_TAPS[c]):
                    if j == 0:
                        if c:
                            act.wait_ge(conv_done, c)
                        dst = acc2
                    else:
                        if c or j > 2:
                            act.wait_ge(tap_added, added_before(c) + max(j - 2, 0))
                        dst = tapp[:, j % 2, :]
                    nc.scalar.activation(dst, upad[:, c % 2, j:j + T], ACT.Copy,
                                         scale=w_dw_c[:, c, j:j + 1]).then_inc(tap_made, 1)
            act.wait_ge(in_done, DC)
            for c in range(DC):
                act.wait_ge(cv_moved, c + 1)
                nc.scalar.activation(hT[:, c, :], cv[:, c, :], ACT.Square).then_inc(squared, 1)
            for half in range(2):
                std = tapp[:, 1, 512 * half:512 * half + 512]
                act.wait_ge(var_kept, half + 1)
                nc.scalar.activation(std, std, ACT.Sqrt, bias=eps[:, :], scale=1.0 / D).then_inc(ln_root, 1)
            for half in range(2):
                for c in range(DC):
                    act.wait_ge(cv_moved, DC * (half + 1) + c + 1)
                    at = slice(512 * half, 512 * half + 512)
                    nc.scalar.activation(hT[:, c, at], cv[:, c, at], ACT.Silu, bias=ln_b_c[:, c:c + 1],
                                         scale=ln_g_c[:, c:c + 1]).then_inc(ln_done, 1)
            for t in range(TT + 1):
                if t < TT:
                    act.wait_ge(out_used, 2 * t + 2)
                    square(3, t)
                    roots(3, t)
                if t >= 1:
                    norm_keep(3, t - 1)
                if t == TT - 1:
                    keep_scores(1, 0)
            moe(1)
            for t in range(TT):
                act.wait_ge(x_added[1], t + 1)
                square(4, t)
                roots(4, t)

        @block.vector
        def _(dve):
            steps = [0]

            def step(ins):
                steps[0] += 1
                ins.then_inc(dve_step, 1)
                dve.wait_ge(dve_step, steps[0])

            V = nc.vector
            for n, dst in enumerate((tokid[:, :], pref_g[:, :, :].rearrange("p t g -> p (t g)"),
                                     pref_e[:, :, :].rearrange("p t e -> p (t e)"))):
                dve.wait_ge(const_made, 3 + n)
                step(V.tensor_copy(dst, iota_i[:, 0:dst.shape[1]]))

            V.tensor_scalar(tile_first[:, :], tokid[:, :], tokid[:, 0:1], None, ALU.subtract)

            def norm_scale(n, t):
                dve.wait_ge(root_done, TT * n + t + 1)
                step(V.reciprocal(rstd[:, t:t + 1], rstd[:, t:t + 1]))
                if n == 4:
                    if t >= 2:
                        dve.wait_ge(out_stored[t % 2], 16 * (t // 2))
                    V.scalar_tensor_tensor(hbuf[t % 2], xtile(t), rstd[:, t:t + 1], bcA[:, :], ALU.mult,
                                           ALU.mult).then_inc(final_made, 1)
                    return
                if t >= 4 and n != 1:
                    dve.wait_ge(h_turned, TT * n + t - 3)
                    if n == 3:
                        dve.wait_ge(h_stored[t % 4], 16 * (TT // 4 + t // 4))
                V.tensor_scalar(hrow(n, t), xtile(t), rstd[:, t:t + 1], None, ALU.mult).then_inc(h_made, 1)

            def norm_keep(n, t):
                dve.wait_ge(h_turned, TT * n + t + 1)
                for c in range(4, DC):
                    ins = V.tensor_scalar(hT[:, c, t * P:(t + 1) * P], bank(2 * (t % 2) + 1)[:, (c - 4) * P:(c - 3) * P],
                                          modc[:, n, 1, c:c + 1], modc[:, n, 0, c:c + 1], ALU.mult, ALU.add)
                ins.then_inc(h_kept2, 1)

            def make_modc(n):
                V.scalar_tensor_tensor(modc[:, n, 1, :], modc[:, n, 1, :], 1.0, norm_c[:, DC * n:DC * (n + 1)],
                                       ALU.add, ALU.mult).then_inc(modc_made, 1)

            for t in range(4):
                norm_scale(0, t)
            dve.wait_ge(cols_loaded, 64)
            for n in range(FIRST_ADA):
                dve.wait_ge(ada_used, n + 1)
                at = kv[0:1, 512 * n:512 * n + 512]
                V.tensor_tensor(at, bank(4 + n)[0:1, :], at, ALU.add).then_inc(ada_row, 1)
            dve.wait_ge(row_turned, 1)
            V.tensor_copy(modc[:, 0, 0, :], bank(4)[:, 0:DC])
            V.scalar_tensor_tensor(modc[:, 0, 1, :], bank(4)[:, DC:2 * DC], 1.0, norm_c[:, 0:DC], ALU.add,
                                   ALU.mult).then_inc(modc_made, 1)
            dve.wait_ge(modc_made, 1)
            for t in range(TT):
                if t >= 4:
                    norm_scale(0, t)
                norm_keep(0, t)
            V.memset(oT[:, :, :], 0.0).then_inc(bias_zeroed, 1)
            dve.wait_ge(h_turned, TT)

            def sum_pieces(i, first=False):
                for u in range(2):
                    dve.wait_ge(ada_loaded[u], 16 * i + 16)
                    dve.wait_ge(bias_loaded[u], 16 * i + 16)
                    if not first:
                        dve.wait_ge(ada_reduced, 2 * i + u - 1)
                    for c in range(DC):
                        if c:
                            dve.wait_ge(ada_step, 14 * i + 7 * u + c)
                        ins = V.scalar_tensor_tensor(ada_sum[:, u, :], vslot[u][:, 512 * c:512 * c + 512],
                                                     cond[:, c:c + 1], ada_sum[:, u, :] if c else bias[:, u, :],
                                                     ALU.mult, ALU.add)
                        ins.then_inc(ada_step if c < DC - 1 else ada_summed, 1)

            sum_pieces(0, first=True)
            with dve.Fori(1, REST_ADA // 2) as i:
                sum_pieces(i)

            def probabilities(qb, g, u, early=False):
                w = (qb + 1) * P
                dve.wait_ge(omega_done, g + 1)
                V.tensor_tensor_scan(pbuf[:, u, D - w:D][:, ::-1], omega[:, u, 0:w][:, ::-1], omega[:, u, 0:w], 1.0,
                                     ALU.mult, ALU.bypass).then_inc(scanned, 1)
                dve.wait_ge(scanned, g + 1)
                dve.wait_ge(sig_done, g + 1)
                if not early:
                    dve.wait_ge(prob_turned, g - 1)
                V.tensor_tensor(prob[:, u, 0:w], beta[:, u, 0:w], pbuf[:, u, D - w + 1:D + 1],
                                ALU.mult).then_inc(prob_made, 1)

            def keep_o(pair, chunk):
                dve.wait_ge(av_done, 2 * pair + 2)
                V.tensor_copy(bcA[:, ds(chunk * P, P)], bank(6)[:, 0:P]).then_inc(o_kept, 1)

            def add_projection(qb):
                dve.wait_ge(wo_done, qb + 1)
                dve.wait_ge(gate_loaded, 16)
                dve.wait_ge(x_again, 16 * (qb + 1))
                V.tensor_tensor(bcA[:, :], bank(4, 2), bcC[:, :], ALU.mult).then_inc(wo_scaled, 1)
                dve.wait_ge(wo_scaled, qb + 1)
                V.tensor_tensor(xq[:, qb, :, :].rearrange("p c j -> p (c j)"), bcA[:, :], bcB[:, :],
                                ALU.add).then_inc(x_made, 1)

            dve.wait_ge(proj_done, 32)
            V.memset(ring[:, 2, 0:D], 0.0).then_inc(zeros_made, 1)
            for qb in range(TT):
                if qb == 1:
                    dve.wait_ge(modc_loaded, 32 * 3)
                    for n in range(1, 4):
                        make_modc(n)
                for u in range(2):
                    probabilities(qb, 16 * qb + u, u, early=(qb == 0))
                if qb:
                    add_projection(qb - 1)
                with dve.Fori(1, HEADS // 2) as i:
                    for u in range(2):
                        probabilities(qb, 16 * qb + 2 * i + u, u)
                    keep_o(8 * qb + i - 1, i - 1)
                keep_o(8 * qb + 7, 7)
            for t in range(TT - 1):
                norm_scale(1, t)
            add_projection(TT - 1)

            def moe(l):
                sc, sel, a, b, m0, m1, both_ = (tmp(n) for n in (0, 1, 2, 3, 4, 5, 6))
                gs, g1, g2, g3 = (tmp(n, GROUPS) for n in (7, 8, 9, 10))
                one = lambda n: tmp(n, 1)

                def wide(ap, w):
                    return ap.to_broadcast([P, TT, w])

                dve.wait_ge(score_done[l], 1)
                dve.wait_ge(cols_loaded, 64)
                score = bank(6)[:, 0:TT * E].rearrange("p (t e) -> p t e", t=TT)
                V.tensor_copy(sc, score)
                step(V.tensor_tensor(sel, score, brt[:, :].unsqueeze(1).to_broadcast([P, TT, E]), ALU.add))
                s4 = sel.rearrange("p t (g e) -> p t g e", e=EPG)
                r = [s4[:, :, :, j] for j in range(EPG)]
                V.tensor_tensor(gs, r[0], r[1], ALU.max)
                V.tensor_tensor(g1, r[0], r[1], ALU.min)
                V.tensor_tensor(g2, r[2], r[3], ALU.max)
                step(V.tensor_tensor(g3, r[2], r[3], ALU.min))
                step(V.tensor_tensor(g1, g1, g3, ALU.max))
                step(V.tensor_tensor(g3, gs, g2, ALU.min))
                step(V.tensor_tensor(gs, gs, g2, ALU.max))
                step(V.tensor_tensor(g1, g1, g3, ALU.max))
                step(V.tensor_tensor(gs, gs, g1, ALU.add))

                def first_largest(dst, src, prefer, w, scratch, top):
                    step(V.tensor_reduce(top, src, AX.X, ALU.max))
                    step(V.tensor_tensor(scratch, src, wide(top, w), ALU.is_equal))
                    step(V.tensor_tensor(scratch, scratch, prefer, ALU.mult))
                    step(V.tensor_reduce(top, scratch, AX.X, ALU.max))
                    step(V.tensor_tensor(dst, scratch, wide(top, w), ALU.is_equal))

                first_largest(g2, gs, pref_g[:, :, :], GROUPS, g1, one(11))
                step(V.tensor_scalar(g3, g2, -1.0, 1e30, ALU.add, ALU.mult))
                a4, w4 = a.rearrange("p t (g e) -> p t g e", e=EPG), [P, TT, GROUPS, EPG]
                for j in range(EPG):
                    V.tensor_tensor(a4[:, :, :, j], r[j], g2, ALU.mult)
                step(V.memset(both_, 0.0))
                for j in range(EPG):
                    ins = V.tensor_tensor(a4[:, :, :, j], a4[:, :, :, j], g3, ALU.add)
                step(ins)
                first_largest(m0, a, pref_e[:, :, :], E, b, one(11))
                step(V.tensor_scalar(b, m0, -1e30, None, ALU.mult))
                step(V.tensor_tensor(a, a, b, ALU.add))
                first_largest(m1, a, pref_e[:, :, :], E, b, one(11))
                step(V.tensor_tensor(both_, m0, m1, ALU.add))
                run = spare[:, 12 * P:12 * P + (TT + 1) * E].rearrange("p (t e) -> p t e", e=E)
                step(V.memset(run[:, 0, :], 0.0))
                for t in range(TT):
                    step(V.tensor_tensor(run[:, t + 1, :], run[:, t, :], both_[:, t, :], ALU.add))
                V.tensor_copy(b, both_).then_inc(picked[l], 1)
                dve.wait_ge(counted[l], 1)
                dest_f, slot_f = dest[:, :, :].rearrange("p k t -> p (k t)"), spare[:, 18 * P:18 * P + 4 * TT].rearrange(
                    "p (h n) -> p h n", h=2)
                cnt, nb, cum, zero = (spare[:, (14 + n) * P:(14 + n) * P + E] for n in range(4))
                step(V.memset(nb, 1.0))
                step(V.memset(zero, 0.0))
                step(V.tensor_copy(cnt, bank(5)[:, P:P + E]))
                for j in range(1, T // P):
                    step(V.scalar_tensor_tensor(nb, cnt, float(j * P), nb, ALU.is_gt, ALU.add))
                step(V.tensor_tensor_scan(cum, nb, zero, 0.0, ALU.add, ALU.add))
                V.memset(bounds[:, :], 0)
                V.tensor_tensor(nb, cum, nb, ALU.subtract).then_inc(dve_step, 1)
                steps[0] += 1
                dve.wait_ge(dve_step, steps[0])
                V.tensor_copy(bounds[:, 1:E + 1], cum[0:1, :]).then_inc(bounds_made[l], 1)
                step(V.tensor_scalar(nb, nb, float(P), None, ALU.mult))
                step(V.tensor_tensor(b, bank(5)[:, 0:P].rearrange("p (t e) -> p t e", t=TT),
                                     nb.unsqueeze(1).to_broadcast([P, TT, E]), ALU.add))
                for k, m in enumerate((m0, m1)):
                    step(V.tensor_tensor(a, b, m, ALU.mult))
                    step(V.tensor_reduce(one(11)[:, :, 0], a, AX.X, ALU.add))
                    step(V.tensor_copy(dest[:, k, :], one(11)[:, :, 0]))
                step(V.tensor_single_scalar(slot_i[:, 0, :], dest_f, P - 1, ALU.bitwise_and))
                step(V.tensor_single_scalar(slot_i[:, 1, :], dest_f, P.bit_length() - 1, ALU.arith_shift_right))
                step(V.tensor_copy(slot_f, slot_i[:, :, :]))
                V.tensor_tensor(low_hot, lane.unsqueeze(1).to_broadcast([P, 2 * TT, P]),
                                slot_f[:, 0, :].unsqueeze(2).to_broadcast([P, 2 * TT, P]), ALU.is_equal)
                step(V.tensor_tensor(high_hot, lane[:, 0:TABLE].unsqueeze(1).to_broadcast([P, 2 * TT, TABLE]),
                                     slot_f[:, 1, :].unsqueeze(2).to_broadcast([P, 2 * TT, TABLE]), ALU.is_equal))
                V.tensor_scalar(high_row, high_hot, tokid[:, 0:1], None, ALU.mult).then_inc(hot_made[l], 1)
                for k in range(2):
                    V.tensor_tensor(high_tile[:, TT * k:TT * (k + 1), :], high_hot[:, TT * k:TT * (k + 1), :],
                                    tile_first[:, :].unsqueeze(2).to_broadcast([P, TT, TABLE]),
                                    ALU.mult).then_inc(hot_made[l], 1)
                dve.wait_ge(table_summed[l], 1)
                V.tensor_copy(slot_tok[:, :], bank(6)[:, 0:TABLE]).then_inc(table_made[l], 1)
                for k, m in enumerate((m0, m1)):
                    step(V.tensor_tensor(a, sc, m, ALU.mult))
                    step(V.tensor_reduce(wts[:, k, :], a, AX.X, ALU.add))
                step(V.tensor_tensor(one(11)[:, :, 0], wts[:, 0, :], wts[:, 1, :], ALU.add))
                step(V.reciprocal(one(11)[:, :, 0], one(11)[:, :, 0]))
                for k in range(2):
                    step(V.tensor_tensor(wts[:, k, :], wts[:, k, :], one(11)[:, :, 0], ALU.mult))

                def keep(b):
                    dve.wait_ge(x_turned[l], b + 1)
                    for c in range(4, DC):
                        ins = V.tensor_scalar(xT[:, c, :], bank(3)[:, (c - 4) * P:(c - 3) * P],
                                              modc[:, 2 * l + 1, 1, c:c + 1], modc[:, 2 * l + 1, 0, c:c + 1],
                                              ALU.mult, ALU.add)
                    ins.then_inc(xT_kept2[l], 1)

                keep(0)
                dve.wait_ge(gate_loaded, 16 * (2 * l + 2))
                blocks = dve.value_load(bounds[0:1, E:E + 1], min_val=1, max_val=MAXBLK)
                with dve.Fori(0, blocks) as n:
                    dve.wait_ge(silu_done[l], n + 1)
                    for f in range(2):
                        dve.wait_ge(up_done[l], 2 * n + f + 1)
                        at = slice(256 * f, 256 * f + 256)
                        V.tensor_tensor(ha[:, at], sg[:, at], bank((1, 7)[f])[:, 0:256], ALU.mult).then_inc(
                            ha_made[l], 1)
                    for f in range(2):
                        dve.wait_ge(ha_turned[l], 2 * n + f + 1)
                        V.tensor_copy(haT[:, 256 * f:256 * f + 256], bank((4, 0)[f])[:, 0:256]).then_inc(haT_kept[l], 1)
                    keep(n + 1)
                    dve.wait_ge(stored[l], 16 * n + 16)
                    for f in range(2):
                        dve.wait_ge(down_done[l], 2 * n + f + 1)
                        V.tensor_tensor(yo[:, 512 * f:512 * f + 512], bank(5 + f), bcC[:, 512 * f:512 * f + 512],
                                        ALU.mult).then_inc(y_kept[l], 1)

            def combine(l, t):
                dve.wait_ge(y_gathered[l][t % 4], 32 * (t // 4 + 1))
                step(V.scalar_tensor_tensor(xtile(t), ygat[t % 4][:, 0, :], wts[:, 0, t:t + 1], xtile(t), ALU.mult,
                                            ALU.add))
                V.scalar_tensor_tensor(xtile(t), ygat[t % 4][:, 1, :], wts[:, 1, t:t + 1], xtile(t), ALU.mult,
                                       ALU.add).then_inc(x_added[l], 1)

            norm_keep(1, 0)
            norm_scale(1, TT - 1)
            for t in range(1, TT):
                norm_keep(1, t)
            dve.wait_ge(const_made, 6)
            V.tensor_copy(lane, iota_i)
            moe(0)
            for t in range(TT + 2):
                if t < TT:
                    combine(0, t)
                if 1 <= t <= TT:
                    norm_scale(2, t - 1)
                if t >= 2:
                    norm_keep(2, t - 2)
            step(V.memset(upad[:, :, 0:CW - 1], 0.0))
            for c in range(DC):
                g = 4 * ((c + 1) % 2)
                dve.wait_ge(usig_done, c + 1)
                u = upad[:, c % 2, :]
                V.scalar_tensor_tensor(u[:, CW - 1:UW], bank(g, 2), b_in_c[:, c:c + 1], usig[:, c % 2, :], ALU.add,
                                       ALU.mult).then_inc(u_done, 1)
                dve.wait_ge(u_done, c + 1)
                first = ADD_TAPS[c]
                step(V.tensor_scalar(cv[:, c, :], u[:, first:first + T], w_dw_c[:, c, first:first + 1],
                                     b_dw_c[:, c:c + 1], ALU.mult, ALU.add))
                for k in range(first + 1, CW - PE_TAPS[c]):
                    step(V.scalar_tensor_tensor(cv[:, c, :], u[:, k:k + T], w_dw_c[:, c, k:k + 1], cv[:, c, :],
                                                ALU.mult, ALU.add))
                if PE_TAPS[c]:
                    dve.wait_ge(taps_summed, sum(n > 0 for n in PE_TAPS[:c + 1]))
                    step(V.tensor_tensor(cv[:, c, :], cv[:, c, :], bank(taps_bank(c), 2), ALU.add))
                dve.wait_ge(tap_added, added_before(c + 1))
                V.tensor_tensor(cv[:, c, :], cv[:, c, :], acc2, ALU.add).then_inc(conv_done, 1)
            dve.wait_ge(ln_summed, 1)
            step(V.tensor_scalar(usig[:, 0, :], bank(6, 2), 1.0 / D, None, ALU.mult))
            step(V.tensor_copy(acc2, usig[:, 0, :]))
            for c in range(DC):
                V.tensor_tensor(cv[:, c, :], cv[:, c, :], acc2, ALU.subtract).then_inc(cv_moved, 1)
            for half in range(2):
                dve.wait_ge(ln_summed, half + 2)
                V.tensor_copy(tapp[:, 1, 512 * half:512 * half + 512], bank(2 + half)).then_inc(var_kept, 1)
            for half in range(2):
                at = slice(512 * half, 512 * half + 512)
                dve.wait_ge(ln_root, half + 1)
                step(V.reciprocal(tapp[:, 1, at], tapp[:, 1, at]))
                for c in range(DC):
                    V.tensor_tensor(cv[:, c, at], cv[:, c, at], tapp[:, 1, at], ALU.mult).then_inc(cv_moved, 1)
            dve.wait_ge(bc_loaded, 16)
            dve.wait_ge(gate_loaded, 16 * 3)
            for t in range(TT):
                for half in range(2):
                    n = 2 * t + half
                    cs = slice(512 * half, 512 * half + 512)
                    dve.wait_ge(out_done, n + 1)
                    y = acc2[:, cs]
                    step(V.tensor_tensor(y, bank(6 + n % 2), tapp[:, 0, cs], ALU.add))
                    step(V.tensor_tensor(y, y, bcC[:, cs], ALU.mult))
                    xt = xq[:, t, 4 * half:4 * half + 4, :].rearrange("p c j -> p (c j)")
                    V.tensor_tensor(xt, xt, y, ALU.add).then_inc(out_used, 1)
                norm_scale(3, t)
                if t:
                    norm_keep(3, t - 1)
            norm_keep(3, TT - 1)
            moe(1)
            dve.wait_ge(bc_loaded, 32)
            for t in range(TT + 1):
                if t < TT:
                    combine(1, t)
                if t:
                    norm_scale(4, t - 1)

        @block.tensor
        def _(pe):
            mm = nc.tensor.matmul
            pe.wait_ge(cond_made, 1)
            for n in range(FIRST_ADA):
                pe.wait_ge(ada_first[n], 16)
                for c in range(DC):
                    ins = mm(bank(4 + n)[0:1, :], cond[:, c:c + 1], ring[:, (n + 2) % 3, 512 * c:512 * c + 512],
                             start=(c == 0), stop=(c == DC - 1))
                ins.then_inc(ada_used, 1)
            def turn(n, t):
                pe.wait_ge(h_made, TT * n + t + 1)
                if t >= 2:
                    pe.wait_ge(h_kept, TT * n + t - 1)
                    pe.wait_ge(h_kept2, TT * n + t - 1)
                for c in range(DC):
                    ins = nc.tensor.transpose(bank(2 * (t % 2), 2)[:, c * P:(c + 1) * P],
                                              hrow(n, t)[:, c * P:(c + 1) * P], ident[:, :])
                ins.then_inc(h_turned, 1)

            def turned(n, t):
                pe.wait_ge(h_kept, TT * n + t + 1)
                pe.wait_ge(h_kept2, TT * n + t + 1)

            def logits(n, t):
                turned(n, t)
                for c in range(DC):
                    ins = mm(bank(4, 2)[0:E, t * P:(t + 1) * P], wr[:, c, :], hT[:, c, t * P:(t + 1) * P],
                             start=(c == 0), stop=(c == DC - 1))
                ins.then_inc(logits_done[n // 2], 1)

            pe.wait_ge(const_made, 2)
            turn(0, 0)
            turn(0, 1)
            pe.wait_ge(ada_row, FIRST_ADA)
            for c in range(2 * DC):
                ins = mm(bank(4)[:, c:c + 1], kv[0:1, c * P:(c + 1) * P], ones[0:1, 0:1], start=True, stop=True)
            ins.then_inc(row_turned, 1)

            for t in range(2, TT // 2 + 2):
                turn(0, t)
            turned(0, TT // 2 - 1)
            reduced = 0
            for cc in range(16):
                j, q = cc // 4, cc % 4
                if q == 0:
                    pe.wait_ge(at_loaded[j], 16)
                if cc >= 2:
                    pe.wait_ge(proj_kept, cc - 1)
                for half in range(2):
                    if cc == 0 and half:
                        for t in range(TT // 2 + 2, TT):
                            turn(0, t)
                        turned(0, TT - 1)
                    for c in range(DC):
                        ins = mm(bank(qk_bank(cc) + half), ring[:, j % 3, 512 * c + P * q:512 * c + P * q + P],
                                 hT[:, c, 512 * half:512 * half + 512], start=(c == 0), stop=(c == DC - 1))
                ins.then_inc(proj_done, 1)
                while reduced < reduced_after(cc) or (cc == 15 and reduced < REST_ADA):
                    pe.wait_ge(ada_summed, reduced + 1)
                    if reduced >= 2:
                        pe.wait_ge(row_kept, reduced - 1)
                    mm(bank(4 + reduced % 2), ones[:, :], ada_sum[:, reduced % 2, :], start=True,
                       stop=True).then_inc(ada_reduced, 1)
                    reduced += 1
            for t in range(TT):
                if t == 0:
                    pe.wait_ge(at_loaded[4], 16)
                    pe.wait_ge(at_loaded[5], 16)
                pe.wait_ge(proj_kept, 15 + t)
                for half in range(2):
                    for c in range(DC):
                        ins = mm(bank(qk_bank(t) + half), hT[:, c, t * P:(t + 1) * P],
                                 ring[:, (4 + half) % 3, 512 * c:512 * c + 512], start=(c == 0), stop=(c == DC - 1))
                    ins.then_inc(proj_done, 1)

            def scores(qb, g, u, chunk, early=False):
                w = (qb + 1) * P
                pe.wait_ge(q_staged, g + 1)
                if not early:
                    pe.wait_ge(sig_done, g - 1)
                for n0 in range(0, w, 512):
                    n1 = min(w, n0 + 512)
                    mm(bank(2 * u, 2)[:, n0:n1], qstage[:, u, :],
                       kT[:, ds(chunk, 1), n0:n1].rearrange("p a t -> p (a t)"), start=True, stop=n1 < w)
                ins = mm(bank(2 * u, 2)[:, w - P:w], identb[:, :], maskb[:, :], start=False, stop=True)
                ins.then_inc(z_done, 1)

            def turn_probabilities(qb, g, u, first=False):
                pe.wait_ge(prob_made, g + 1)
                if first and qb:
                    pe.wait_ge(wo_scaled, qb)
                if not first or qb:
                    pe.wait_ge(probT_kept, g)
                for s in range(qb + 1):
                    ins = nc.tensor.transpose(bank(4, 2)[:, s * P:(s + 1) * P], prob[:, u, s * P:(s + 1) * P],
                                              ident[:, :])
                ins.then_inc(prob_turned, 1)

            def values(qb, g, u, chunk, pair):
                pe.wait_ge(probT_kept, g + 1)
                if u == 0 and pair is not None:
                    pe.wait_ge(o_kept, pair)
                for s in range(qb + 1):
                    ins = mm(bank(6)[:, HD * u:HD * u + HD], probT[:, u, s * P:(s + 1) * P],
                             vt[:, s, ds(chunk * P + HD * u, HD)], start=(s == 0), stop=(s == qb))
                ins.then_inc(av_done, 1)

            def turn_outputs(qb, half, at):
                pe.wait_ge(o_kept, 8 * qb + 4 * half + 4)
                for c in range(4):
                    ins = nc.tensor.transpose(bank(at)[:, c * P:(c + 1) * P],
                                              bcA[:, (4 * half + c) * P:(4 * half + c + 1) * P], ident[:, :])
                ins.then_inc(o_turned, 1)

            pe.wait_ge(proj_kept, 24)
            scores(0, 0, 0, 0, early=True)
            scores(0, 1, 1, 0, early=True)
            for qb in range(TT):
                last = qb == TT - 1
                g = 16 * qb
                scores(qb, g + 2, 0, 1)
                turn_probabilities(qb, g, 0, first=True)
                scores(qb, g + 3, 1, 1)
                turn_probabilities(qb, g + 1, 1)
                values(qb, g, 0, 0, 8 * qb if qb else None)
                with pe.Fori(1, HEADS // 2 - 1) as i:
                    gi = g + 2 * i
                    scores(qb, gi + 2, 0, i + 1)
                    turn_probabilities(qb, gi, 0)
                    values(qb, gi - 1, 1, i - 1, None)
                    scores(qb, gi + 3, 1, i + 1)
                    turn_probabilities(qb, gi + 1, 1)
                    values(qb, gi, 0, i, 8 * qb + i)
                if not last:
                    scores(qb + 1, g + 16, 0, 0)
                turn_probabilities(qb, g + 14, 0)
                values(qb, g + 13, 1, 6, None)
                if not last:
                    scores(qb + 1, g + 17, 1, 0)
                turn_probabilities(qb, g + 15, 1)
                turn_outputs(qb, 0, 7)
                values(qb, g + 14, 0, 7, 8 * qb + 7)
                values(qb, g + 15, 1, 7, None)
                turn_outputs(qb, 1, 6)
                if qb == 0:
                    pe.wait_ge(at_loaded[6], 16)
                    pe.wait_ge(at_loaded[7], 16)
                for half in range(2):
                    for c in range(DC):
                        if half == 0 and c % 4 == 0:
                            pe.wait_ge(oT_kept, 2 * qb + c // 4 + 1)
                        ins = mm(bank(4 + half), oT[:, c, :], ring[:, half, 512 * c:512 * c + 512],
                                 start=(c == 0), stop=(c == DC - 1))
                ins.then_inc(wo_done, 1)

            def moe(l):
                pe.wait_ge(scT_made[l], 2)
                for t in range(TT):
                    ins = nc.tensor.transpose(bank(6)[:, E * t:E * t + E], scT[:, t * P:(t + 1) * P],
                                              ident[0:E, 0:E])
                ins.then_inc(score_done[l], 1)
                pe.wait_ge(picked[l], 1)
                run = spare[:, 12 * P:12 * P + (TT + 1) * E]
                mm(bank(5)[:, 0:P], upper[:, :], spare[:, 6 * P:7 * P], start=True, stop=False)
                mm(bank(5)[:, 0:P], ones[:, :], run[:, 0:P], start=False, stop=True)
                mm(bank(5)[:, P:P + E], ones[:, :], run[:, P:P + E], start=True, stop=True).then_inc(counted[l], 1)
                pe.wait_ge(hot_made[l], 3)
                for n in range(2 * TT):
                    mm(bank(6)[:, 0:TABLE], low_hot[:, n, :], high_row[:, n, :], start=(n == 0), stop=False)
                    ins = mm(bank(6)[:, 0:TABLE], low_hot[:, n, :], high_tile[:, n, :], start=False,
                             stop=(n == 2 * TT - 1))
                ins.then_inc(table_summed[l], 1)

                def turn_rows(b, f):
                    if f == 0:
                        pe.wait_ge(x_gathered[l], 16 * b + 16)
                    for c in range(4 * f, 4 * f + 4):
                        ins = nc.tensor.transpose(bank(2, 2)[:, c * P:(c + 1) * P], xg[:, c * P:(c + 1) * P],
                                                  ident[:, :])
                    if f:
                        ins.then_inc(x_turned[l], 1)

                turn_rows(0, 0)
                turn_rows(0, 1)
                with pe.Fori(0, E // 2) as i:
                    for s in range(2):
                        wg, wu, wd = wset[s]
                        first = pe.value_load(bounds[0:1, ds(2 * i + s, 1)], min_val=0, max_val=MAXBLK)
                        end = pe.value_load(bounds[0:1, ds(2 * i + s + 1, 1)], min_val=1, max_val=MAXBLK)
                        with pe.Fori(first, end) as b:
                            pe.wait_ge(xT_kept[l], b + 1)
                            pe.wait_ge(xT_kept2[l], b + 1)
                            pe.wait_ge(w_loaded[l][s][0], 16 * i + 16)
                            for c in range(DC):
                                ins = mm(bank(0), xT[:, c, :], wg[:, F * c:F * c + F],
                                         start=(c == 0), stop=(c == DC - 1))
                            ins.then_inc(gate_done[l], 1)
                            pe.wait_ge(w_loaded[l][s][1], 16 * i + 16)
                            for f in range(2):
                                for c in range(DC):
                                    ins = mm(bank((1, 7)[f])[:, 0:256], xT[:, c, :],
                                             wu[:, F * c + 256 * f:F * c + 256 * f + 256],
                                             start=(c == 0), stop=(c == DC - 1))
                                ins.then_inc(up_done[l], 1)
                            for f in range(2):
                                pe.wait_ge(ha_made[l], 2 * b + f + 1)
                                for c in range(2):
                                    at = 256 * f + P * c
                                    ins = nc.tensor.transpose(bank((4, 0)[f])[:, c * P:(c + 1) * P], ha[:, at:at + P],
                                                              ident[:, :])
                                ins.then_inc(ha_turned[l], 1)
                                turn_rows(b + 1, f)
                            pe.wait_ge(w_loaded[l][s][2], 16 * i + 16)
                            pe.wait_ge(haT_kept[l], 2 * b + 2)
                            for half in range(2):
                                for c in range(F // P):
                                    ins = mm(bank(5 + half), haT[:, c * P:(c + 1) * P],
                                             wd[:, D * c + 512 * half:D * c + 512 * half + 512],
                                             start=(c == 0), stop=(c == F // P - 1))
                                ins.then_inc(down_done[l], 1)

            for t in range(TT):
                turn(1, t)
                if t:
                    logits(1, t - 1)
            logits(1, TT - 1)
            moe(0)
            for t in range(TT // 2):
                turn(2, t)
            turned(2, TT // 2 - 1)
            for c in range(DC):
                g = 4 * ((c + 1) % 2)
                if c % 4 == 0:
                    pe.wait_ge(cv_loaded[c // 2], 16)
                    pe.wait_ge(cv_loaded[c // 2 + 1], 16)
                if c >= 2:
                    pe.wait_ge(u_done, c - 1)
                for n, (half, part) in enumerate(((0, 0), (0, 1), (1, 0), (1, 1)) if c == 0 else
                                                 ((0, 0), (1, 0), (0, 1), (1, 1))):
                    if c == 0 and n < 2:
                        turn(2, TT // 2 + n)
                    if c == 0 and n == 2:
                        for t in range(TT // 2 + 2, TT):
                            turn(2, t)
                        turned(2, TT - 1)
                    slot = (2 * (c // 4) + part) % 3
                    for k in range(DC):
                        ins = mm(bank(g + 2 * part + half),
                                 ring[:, slot, 512 * k + P * (c % 4):512 * k + P * (c % 4) + P],
                                 hT[:, k, 512 * half:512 * half + 512], start=(k == 0), stop=(k == DC - 1))
                    if (half, part) == (1, 0):
                        ins.then_inc(values_done, 1)
                ins.then_inc(in_done, 1)
            def sum_taps(c):
                pe.wait_ge(diag_made, 1)
                pe.wait_ge(u_done, c + 1)
                mine = [n for n in range(sum(PE_TAPS)) if diag_chunk[n] == c]
                for half in range(2):
                    for n in mine:
                        at = diag_tap[n] + 512 * half
                        ins = mm(bank(taps_bank(c) + half), diag(n), upad[:, c % 2, at:at + 512],
                                 start=(n == mine[0]), stop=(n == mine[-1]))
                ins.then_inc(taps_summed, 1)

            def sum_chunks(chunks):
                for c in chunks:
                    pe.wait_ge(conv_done, c + 1)
                    for half in range(2):
                        ins = mm(bank(6 + half), ones[:, :], cv[:, c, 512 * half:512 * half + 512],
                                 start=(c == 0), stop=(c == DC - 1), skip_group_check=True)
                return ins

            sum_taps(DC - 2)
            sum_chunks(range(DC - 2))
            sum_taps(DC - 1)
            sum_chunks(range(DC - 2, DC)).then_inc(ln_summed, 1)
            for half in range(2):
                for c in range(DC):
                    if half == 0:
                        pe.wait_ge(squared, c + 1)
                    ins = mm(bank(2 + half), ones[:, :], hT[:, c, 512 * half:512 * half + 512],
                             start=(c == 0), stop=(c == DC - 1))
                ins.then_inc(ln_summed, 1)
            pe.wait_ge(cv_loaded[4], 16)
            pe.wait_ge(cv_loaded[5], 16)
            for t in range(TT):
                if t % (TT // 2) == 0:
                    pe.wait_ge(ln_done, DC * (1 + 2 * t // TT))
                for half in range(2):
                    n = 2 * t + half
                    if n >= 2:
                        pe.wait_ge(out_used, n - 1)
                    for c in range(DC):
                        ins = mm(bank(6 + n % 2), hT[:, c, t * P:(t + 1) * P],
                                 ring[:, (4 + half) % 3, 512 * c:512 * c + 512], start=(c == 0), stop=(c == DC - 1))
                    ins.then_inc(out_done, 1)
                if t >= 1:
                    turn(3, t - 1)
                if t >= 2:
                    logits(3, t - 2)
            turn(3, TT - 1)
            logits(3, TT - 2)
            logits(3, TT - 1)
            moe(1)


def kernel(**inputs):
    import numpy as np
    import concourse.bacc as bacc
    from concourse.bass_utils import run_bass_kernel_spmd

    a = {k: np.asarray(v) for k, v in inputs.items()}

    def pieces(w, k, order=None):
        w = w.reshape(-1, k, P, w.shape[-1] // 512, 512).transpose(0, 3, 2, 1, 4)
        w = w.reshape(-1, P, k * 512)
        return np.ascontiguousarray(w if order is None else w[order])

    def col(v):
        return v.reshape(-1, P).T

    def rows(w, k):
        return np.ascontiguousarray(w.reshape(-1, k, P, w.shape[-1]).transpose(0, 2, 1, 3)).reshape(-1, P, k * w.shape[-1])

    dw = a["cv_w_dw"][0].reshape(CW, DC, P).transpose(2, 1, 0).reshape(P, DC * CW)
    data = {
        "x": a["x"].reshape(T, D),
        "c_col": col(a["c"]),
        "b_ada": a["b_ada"].reshape(1, -1),
        "final_g": a["final_g"],
        "vec_cols": np.concatenate([col(a["c"]), col(a["cv_b_in"]), dw, col(a["cv_b_dw"]), col(a["cv_ln_g"]),
                                    col(a["cv_ln_b"])]
                                   + [col(a[f"norm{k}_g"][l]) for l in range(2) for k in (1, 2)], axis=1),
        "b_out": a["cv_b_out"].reshape(D),
        "b_router": a["b_router"],
        "w_router": a["w_router"].reshape(DC, P, E).transpose(1, 0, 2),
        "w_ada": pieces(a["w_ada"], DC),
        "w_qkv": pieces(a["sb_w_qkv"], DC),
        "w_o": pieces(a["sb_w_o"], DC),
        "w_in": pieces(a["cv_w_in"], DC, [0, 2, 1, 3]),
        "w_out": pieces(a["cv_w_out"], DC),
        "w_gate": rows(a["moe_w_gate"], DC),
        "w_up": rows(a["moe_w_up"], DC),
        "w_down": rows(a["moe_w_down"], F // P),
    }
    nc = bacc.Bacc("TRN2", target_bir_lowering=False, num_devices=1)
    arrays, args = {}, []
    for name, v in data.items():
        v = np.ascontiguousarray(v)
        arrays[f"in_{name}"] = v
        args.append(nc.dram_tensor(f"in_{name}", v.shape, mybir.dt.from_np(v.dtype), kind="ExternalInput").ap())
    out = nc.dram_tensor("out_x", (T, D), mybir.dt.float32, kind="ExternalOutput").ap()
    trunk(nc, *args, out)
    r = run_bass_kernel_spmd(nc, [arrays], core_ids=[0])
    return r.results[0]["out_x"].reshape(1, T, D)
```
